# Optimizing a Trainium2 kernel written in Bass

```python
import jax, jax.numpy as jnp
from jax import lax
import numpy as np

D_MODEL = 1024
BATCH = 1
SEQ = 2048
DEPTH = 1

D_MIX = D_MODEL
GLA_HEADS = 4
GLA_DV = 128
GLA_DK = 64
GLA_KEY = GLA_HEADS * GLA_DK
GLA_VAL = GLA_HEADS * GLA_DV
GATE_RANK = 16
GATE_TAU = 16.0
CHUNK = 64
CONV_CH = D_MIX - GLA_VAL
CONV_GROUPS = 8
CONV_W = 31
D_FF = 4 * D_MODEL
EPS = 1e-6

OFF_Q = 0
OFF_K = OFF_Q + GLA_KEY
OFF_V = OFF_K + GLA_KEY
OFF_G = OFF_V + GLA_VAL
OFF_A = OFF_G + GLA_VAL
OFF_C = OFF_A + GATE_RANK
D_IN = OFF_C + 2 * CONV_CH

kernel_name = "hybrid_gla_conformer_conv_block"

def rmsnorm(x, g):
    xf = x.astype(jnp.float32)
    y = xf * lax.rsqrt(jnp.mean(xf * xf, axis=-1, keepdims=True) + EPS)
    return (y * g.astype(jnp.float32)).astype(x.dtype)

def gla_chunked(q, k, v, log_a):
    B, S, H, DK = q.shape
    DV = v.shape[-1]
    nc = S // CHUNK

    def to_chunks(t):
        return t.astype(jnp.float32).reshape(B, nc, CHUNK, H, t.shape[-1]).transpose(1, 0, 3, 2, 4)

    qc, kc, vc, ac = map(to_chunks, (q, k, v, log_a))
    bc = jnp.cumsum(ac, axis=3)
    causal = jnp.tril(jnp.ones((CHUNK, CHUNK), dtype=bool))

    def step(state, inp):
        qi, ki, vi, bi = inp
        o_inter = jnp.einsum('bhcd,bhde->bhce', qi * jnp.exp(bi), state)
        diff = bi[:, :, :, None, :] - bi[:, :, None, :, :]
        decay = jnp.exp(jnp.where(causal[:, :, None], diff, -jnp.inf))
        scores = jnp.einsum('bhid,bhjd,bhijd->bhij', qi, ki, decay)
        o_intra = jnp.einsum('bhij,bhje->bhie', scores, vi)
        b_last = bi[:, :, -1, :]
        k_dec = ki * jnp.exp(b_last[:, :, None, :] - bi)
        new_state = jnp.exp(b_last)[..., None] * state + jnp.einsum('bhcd,bhce->bhde', k_dec, vi)
        return new_state, o_inter + o_intra

    s0 = jnp.zeros((B, H, DK, DV), jnp.float32)
    _, o = lax.scan(step, s0, (qc, kc, vc, bc))
    return o.transpose(1, 0, 3, 2, 4).reshape(B, S, H, DV).astype(v.dtype)

def causal_depthwise_conv(u, w, b):
    u_pad = jnp.pad(u, ((0, 0), (CONV_W - 1, 0), (0, 0)))
    y = lax.conv_general_dilated(
        u_pad, w[:, None, :].astype(u.dtype), window_strides=(1,), padding='VALID',
        dimension_numbers=('NWC', 'WIO', 'NWC'), feature_group_count=u.shape[-1])
    return y + b.astype(u.dtype)

def channel_group_norm(u, g, b):
    B, S, C = u.shape
    uf = u.astype(jnp.float32).reshape(B, S, CONV_GROUPS, C // CONV_GROUPS)
    mu = jnp.mean(uf, axis=-1, keepdims=True)
    var = jnp.mean(jnp.square(uf - mu), axis=-1, keepdims=True)
    y = ((uf - mu) * lax.rsqrt(var + EPS)).reshape(B, S, C)
    return (y * g.astype(jnp.float32) + b.astype(jnp.float32)).astype(u.dtype)

def setup_inputs(seed: int = 0) -> dict:
    key = jax.random.key(seed)
    ks = jax.random.split(key, 16)
    f32 = jnp.float32
    nrm = lambda k, shape, s: jax.random.normal(k, shape, f32) * s
    return {
        "x": jax.random.normal(ks[0], (BATCH, SEQ, D_MODEL), f32),
        "norm1_g": 1.0 + nrm(ks[1], (DEPTH, D_MODEL), 0.02),
        "w_in": nrm(ks[2], (DEPTH, D_MODEL, D_IN), D_MODEL ** -0.5),
        "w_gate_up": nrm(ks[3], (DEPTH, GATE_RANK, GLA_KEY), GATE_RANK ** -0.5),
        "b_gate": nrm(ks[4], (DEPTH, GLA_KEY), 0.1),
        "gla_norm_g": 1.0 + nrm(ks[5], (DEPTH, GLA_DV), 0.02),
        "conv_w": nrm(ks[6], (DEPTH, CONV_W, CONV_CH), CONV_W ** -0.5),
        "conv_b": nrm(ks[7], (DEPTH, CONV_CH), 0.02),
        "conv_norm_g": 1.0 + nrm(ks[8], (DEPTH, CONV_CH), 0.02),
        "conv_norm_b": nrm(ks[9], (DEPTH, CONV_CH), 0.02),
        "w_out": nrm(ks[10], (DEPTH, D_MIX, D_MODEL), D_MIX ** -0.5),
        "norm2_g": 1.0 + nrm(ks[11], (DEPTH, D_MODEL), 0.02),
        "w_mlp_in": nrm(ks[12], (DEPTH, D_MODEL, D_FF), D_MODEL ** -0.5),
        "w_mlp_out": nrm(ks[13], (DEPTH, D_FF, D_MODEL), D_FF ** -0.5),
        "final_norm_g": 1.0 + nrm(ks[14], (D_MODEL,), 0.02),
    }

def reference(x, norm1_g, w_in, w_gate_up, b_gate, gla_norm_g, conv_w, conv_b,
              conv_norm_g, conv_norm_b, w_out, norm2_g, w_mlp_in, w_mlp_out,
              final_norm_g):
    B, S, _ = x.shape
    h = x
    for l in range(DEPTH):
        xn = rmsnorm(h, norm1_g[l])
        proj = jnp.einsum('bsd,de->bse', xn, w_in[l])

        q = proj[..., OFF_Q:OFF_K].reshape(B, S, GLA_HEADS, GLA_DK) * (GLA_DK ** -0.5)
        k = proj[..., OFF_K:OFF_V].reshape(B, S, GLA_HEADS, GLA_DK)
        v = proj[..., OFF_V:OFF_G].reshape(B, S, GLA_HEADS, GLA_DV)
        g = proj[..., OFF_G:OFF_A]
        z = proj[..., OFF_A:OFF_C]
        a_logit = jnp.einsum('bsr,rk->bsk', z, w_gate_up[l]) + b_gate[l]
        log_a = (jax.nn.log_sigmoid(a_logit.astype(jnp.float32)) / GATE_TAU).reshape(B, S, GLA_HEADS, GLA_DK)
        o_gla = gla_chunked(q, k, v, log_a)
        o_gla = rmsnorm(o_gla, gla_norm_g[l]).reshape(B, S, GLA_VAL) * jax.nn.silu(g)

        c_in = proj[..., OFF_C:OFF_C + CONV_CH]
        c_gate = proj[..., OFF_C + CONV_CH:D_IN]
        u = c_in * jax.nn.sigmoid(c_gate)
        u = causal_depthwise_conv(u, conv_w[l], conv_b[l])
        o_conv = jax.nn.silu(channel_group_norm(u, conv_norm_g[l], conv_norm_b[l]))

        mixed = jnp.concatenate([o_gla, o_conv], axis=-1)
        h = h + jnp.einsum('bse,ed->bsd', mixed, w_out[l])

        hn = rmsnorm(h, norm2_g[l])
        ff = jnp.square(jax.nn.relu(jnp.einsum('bsd,df->bsf', hn, w_mlp_in[l])))
        h = h + jnp.einsum('bsf,fd->bsd', ff, w_mlp_out[l])
    return rmsnorm(h, final_norm_g)


_drawn_inputs = setup_inputs


def setup_inputs(seed=0):
    import zlib

    import numpy as np

    out = dict(_drawn_inputs(seed))
    spreads = {}
    factors = {'norm1_g': 2.837,
     'b_gate': 3.227,
     'gla_norm_g': 6.154,
     'conv_b': 12.181,
     'conv_norm_g': 46.253,
     'conv_norm_b': 46.171,
     'norm2_g': 9.822,
     'final_norm_g': 8.237}
    for name, (base, spread) in spreads.items():
        noise = np.random.default_rng([zlib.crc32(name.encode()), seed]).standard_normal(out[name].shape)
        drawn = base * np.exp(spread * noise) if base else spread * noise
        out[name] = __import__('jax').numpy.asarray(drawn.astype(out[name].dtype))
    for name, factor in factors.items():
        out[name] = (out[name] * factor).astype(out[name].dtype)
    return out
```

```python
from contextlib import ExitStack

import concourse.bass as bass
from concourse import mybir

F32 = mybir.dt.float32
F32R = mybir.dt.float32r
BF16 = mybir.dt.bfloat16
I32 = mybir.dt.int32
ALU = mybir.AluOpType
ACT = mybir.ActivationFunctionType

P = 128
D_MODEL = 1024
SEQ = 2048
HEADS = 4
DV = 128
DK = 64
KEY = HEADS * DK
VAL = HEADS * DV
RANK = 16
TAU = 16.0
CONV_CH = D_MODEL - VAL
CONV_GROUP = CONV_CH // 8
TAPS = 31
HALO = TAPS - 1
D_FF = 4 * D_MODEL
EPS = 1e-6
OFF_Q = 0
OFF_K = OFF_Q + KEY
OFF_V = OFF_K + KEY
OFF_G = OFF_V + VAL
OFF_A = OFF_G + VAL
OFF_C = OFF_A + RANK

KT = D_MODEL // P
BLK = 512
NB = SEQ // BLK
TT = BLK // P
CT = CONV_CH // P
PAIRS = HEADS // 2
LEVELS = [64, 32, 16, 8, 4, 2, 1]
NL = len(LEVELS)
NE = NL + 2

UNIT = 512
STAGES = 4
SLOTS = 4
FRONT_UNITS = 2 * 2 * CT + 2 * (KEY // P) * 2 + KT + 2 * HEADS
OUT_UNITS = 2 * KT
BODY_UNITS = FRONT_UNITS + OUT_UNITS

HALF = 1024
NH = SEQ // HALF
HT = HALF // P
FC = 256
FT = FC // P
NF = D_FF // FC


def three_products(nc, out, w_hi, w_lo, x_hi, x_lo, first, last):
    nc.tensor.matmul(out, w_hi, x_hi, start=first, stop=False)
    nc.tensor.matmul(out, w_hi, x_lo, start=False, stop=False)
    return nc.tensor.matmul(out, w_lo, x_hi, start=False, stop=last)


def front_steps(mix, prep):
    unit = 0

    def units(name, arg, n):
        nonlocal unit
        out = [(name, arg, unit, n)]
        unit += n
        return out

    def taps(n):
        nonlocal tap
        out = [("taps", k) for k in range(tap, min(tap + n, TAPS))]
        tap = min(tap + n, TAPS)
        return out

    tap = 0
    s = []
    m = (lambda *x: [x]) if mix else (lambda *x: [])
    s += units("conv_gate", 0, 2) + m("cn_mean") + m("gla_factors", 0)
    s += units("conv_in", 0, 2) + m("cn_var")
    s += units("conv_gate", 1, 2) + m("cn_rstd")
    s += units("conv_in", 1, 2) + m("gla_scores", 0) + m("gla_factors", 1)
    s += units("conv_gate", 2, 2) + m("gla_select", 0)
    s += m("gla_out", 0)
    s += units("conv_in", 2, 2) + m("gla_scores", 1) + m("gla_factors", 2)
    s += units("conv_gate", 3, 2) + m("cn_mixed") + m("gla_select", 1)
    s += m("gla_out", 1)
    s += units("conv_in", 3, 2) + m("gla_scores", 2) + m("gla_factors", 3)
    s += [("z",)] + m("gla_select", 2)
    s += units("qk", 0, 2) + m("gla_out", 2) + m("gla_scores", 3) + taps(1)
    s += [("gate", 0)] + m("gla_select", 3)
    s += units("qk", 1, 2) + taps(1)
    s += [("gate", 1)] + m("gla_out", 3)
    s += units("qk", 2, 2) + m("gn_square") + taps(2)
    s += [("decay",)]
    s += units("qk", 3, 2) + m("gn_sum") + m("gn_rstd") + taps(2)
    for k in range(KT):
        s += units("v", k, 1) + taps(1)
        if k == 3:
            s += m("gn_mixed")
    s += [("v_done", unit - 1)]
    for h in range(HEADS):
        s += units("g", h, 2) + taps(2)
    for half in range(2):
        for k in range(KT):
            if mix:
                s += units("out", (half, k), 1)
            if prep and half == 0 and k in (1, 3):
                s += [("x_prep", k // 2)]
            if prep and half == 1 and k in (1, 3):
                s += [("x_prep", 2 + k // 2)]
            s += taps(1)
        if mix:
            s += [("out_done", half, unit - 1)]
    s += taps(TAPS)
    return s


def mixer_block(nc, x, norm1_g, w_in, w_gate_up, b_gate, gla_norm_g, conv_w, conv_b,
                conv_norm_g, conv_norm_b, w_out, h_dram):
    with ExitStack() as ctx:
        def sb(name, shape, dt=F32):
            return ctx.enter_context(nc.sbuf_tensor(name, shape, dt))

        def sem(name):
            return ctx.enter_context(nc.semaphore(name))

        x_nat = sb("x_nat", [P, 2, D_MODEL])
        junk = sb("junk", [P, D_MODEL], BF16)
        g1_row = sb("g1_row", [P, D_MODEL])
        ssq = sb("ssq", [P, TT])
        rstd = sb("rstd", [P, TT])
        neg_half = sb("neg_half", [P, 1])
        eps_col = sb("eps_col", [P, 1])
        inv_d = sb("inv_d", [P, 1])
        pace = sb("pace", [P, 1])
        one_col = sb("one_col", [P, 1])
        xT_hi = sb("xT_hi", [P, KT, BLK], F32R)
        xT_lo = sb("xT_lo", [P, KT, BLK], F32R)
        w_raw = sb("w_raw", [P, STAGES, UNIT])
        w_hi = sb("w_hi", [P, SLOTS, UNIT], F32R)
        w_lo = sb("w_lo", [P, SLOTS, UNIT], F32R)
        wz_raw = sb("wz_raw", [P, KT, RANK])
        wz = sb("wz", [P, KT, 2, RANK], F32R)
        w_up = sb("w_up", [2 * RANK, KEY])
        bg_col = sb("bg_col", [P, PAIRS])
        z_sb = sb("z_sb", [2 * RANK, BLK])
        q_sb = sb("q_sb", [P, PAIRS, BLK])
        k_sb = sb("k_sb", [P, PAIRS, BLK])
        cum = sb("cum", [P, PAIRS, BLK])
        v_sb = sb("v_sb", [P, TT, VAL])
        silu_g = sb("silu_g", [P, HEADS, BLK])
        sig = sb("sig", [P, 2, BLK])
        log1p_t = sig
        u_sb = sb("u_sb", [P, CT, HALO + BLK])
        y_sb = sb("y_sb", [P, CT, BLK])
        nr = sb("nr", [P, 4, BLK])
        o_sb = sb("o_sb", [P, HEADS, BLK])
        res = o_sb
        mix_hi = sb("mix_hi", [P, KT, BLK], F32R)
        mix_lo = sb("mix_lo", [P, KT, BLK], F32R)
        fac = sb("fac", [P, NE, PAIRS, P])
        ke = sb("ke", [P, NL, PAIRS, P])
        qe = sb("qe", [P, NL, PAIRS, P // 2])
        k_end = sb("k_end", [P, PAIRS, P])
        q_in = sb("q_in", [P, 2, PAIRS, P])
        decay = sb("decay", [P, 2, PAIRS])
        qk = sb("qk", [P, PAIRS, P])
        k_endT = sb("k_endT", [P, PAIRS, P])
        probs = sb("probs", [P, HEADS, P])
        state = sb("state", [P, HEADS, DV])
        lvl_mask = sb("lvl_mask", [P, NL, P // 2])
        ident = sb("ident", [P, P])
        mean_dv = sb("mean_dv", [P, P])
        mean_grp = sb("mean_grp", [P, P])
        cw_col = sb("cw_col", [P, CT, TAPS])
        cb_col = sb("cb_col", [P, CT])
        cg_col = sb("cg_col", [P, CT])
        cnb_col = sb("cnb_col", [P, CT])
        gn_col = sb("gn_col", [P, 1])
        acc = ctx.enter_context(nc.psum_tensor("acc", [P, 8, 512], F32))

        consts_ld = sem("consts_ld")
        made = sem("made")
        w_ld = [sem(f"w_ld{i}") for i in range(STAGES)]
        w_hi_ok = sem("w_hi_ok")
        w_lo_ok = sem("w_lo_ok")
        w_used = sem("w_used")
        wz_ok = sem("wz_ok")
        x_ld = [sem(f"x_ld{i}") for i in range(2)]
        x_ssq = sem("x_ssq")
        x_rstd = sem("x_rstd")
        x_norm = sem("x_norm")
        xt_pe = sem("xt_pe")
        xt_hi_ok = sem("xt_hi_ok")
        low_sum_ok = sem("low_sum_ok")
        z_pe = sem("z_pe")
        gate_pe = sem("gate_pe")
        csig_ok = sem("csig_ok")
        u_ok = sem("u_ok")
        z_ok = sem("z_ok")
        gate_act = sem("gate_act")
        gate_min = sem("gate_min")
        cum_ok = sem("cum_ok")
        qk_ok = sem("qk_ok")
        v_ok = sem("v_ok")
        gsig_ok = sem("gsig_ok")
        silu_ok = sem("silu_ok")
        tap_ok = sem("tap_ok")
        cn_mean_pe, cn_dev, cn_sq, cn_var_pe, cn_rs, cn_n, cn_sig, cn_aff, cn_f, cn_hi, cn_lo = (
            sem(n) for n in ("cn_mean_pe", "cn_dev", "cn_sq", "cn_var_pe", "cn_rs", "cn_n",
                             "cn_sig", "cn_aff", "cn_f", "cn_hi", "cn_lo"))
        gn_sq, gn_sum_pe, gn_rs, gn_n, gn_f, gn_hi, gn_lo = (
            sem(n) for n in ("gn_sq", "gn_sum_pe", "gn_rs", "gn_n", "gn_f", "gn_hi", "gn_lo"))
        expo_ok = sem("expo_ok")
        fac_ok = sem("fac_ok")
        ke_ok = sem("ke_ok")
        score_pe = sem("score_pe")
        kT_pe = sem("kT_pe")
        kT_ok = sem("kT_ok")
        probs_ok = sem("probs_ok")
        o_pe = sem("o_pe")
        o_ok = sem("o_ok")
        upd_pe = sem("upd_pe")
        state_ok = sem("state_ok")
        out_pe = sem("out_pe")
        res_ld = sem("res_ld")
        h_st = sem("h_st")

        block = ctx.enter_context(nc.Block())

        PRO = front_steps(False, True)
        BODY = front_steps(True, True)
        LAST = front_steps(True, False)
        TAIL = [("cn_mean",), ("gla_factors", 0), ("cn_var",), ("cn_rstd",)]
        for c in range(TT):
            TAIL += [("gla_scores", c)] + ([("gla_factors", c + 1)] if c + 1 < TT else [("cn_mixed",)])
            TAIL += [("gla_select", c), ("gla_out", c)]
        TAIL += [("gn_square",), ("gn_sum",), ("gn_rstd",), ("gn_mixed",)]
        for half in range(2):
            TAIL += [("out", (half, k), half * KT + k, 1) for k in range(KT)]
            TAIL += [("out_done", half, half * KT + KT - 1)]

        def base(b):
            return 0 if isinstance(b, int) and b == 0 else b * BODY_UNITS - OUT_UNITS

        def run(eng, do):
            for s in PRO:
                do(s, 0)
            with eng.Fori(1, NB - 1) as b:
                for s in BODY:
                    do(s, b)
            for s in LAST:
                do(s, NB - 1)
            for s in TAIL:
                do(s, NB)

        LAST_UNIT = NB * BODY_UNITS
        assert (FRONT_UNITS % STAGES, OUT_UNITS % STAGES) == (0, 0)

        def first(b):
            return isinstance(b, int) and b == 0

        GROUPS = 2 * TT

        def low_sum_start(b):
            if first(b):
                return GROUPS
            return b * 2 * GROUPS if not (isinstance(b, int) and b == NB) else (b * 2 - 1) * GROUPS

        def low_n(b, t):
            between = 0 if first(b) or t < TT // 2 else TT
            return low_sum_start(b) + 2 * (t + 1) + between

        def sum_n(b, half, t):
            preps = 0 if isinstance(b, int) and b >= NB - 1 else (half + 1) * TT
            return low_sum_start(b) + preps + half * TT + t + 1

        w_in_t = w_in.rearrange("(k p) e -> p k e", p=P)
        w_out_t = w_out.rearrange("(k p) e -> p k e", p=P)
        x_t = x.rearrange("(n p) d -> p n d", p=P)
        h_t = h_dram.rearrange("(n p) d -> p n d", p=P)

        def sources():
            out = []
            for step in BODY:
                name = step[0]
                if name in ("conv_gate", "conv_in", "qk", "g"):
                    off = {"conv_gate": OFF_C + CONV_CH, "conv_in": OFF_C, "qk": OFF_Q, "g": OFF_G}[name] + step[1] * P
                    out += [w_in_t[:, i * 4:i * 4 + 4, off:off + P] for i in range(2)]
                elif name == "v":
                    out += [w_in_t[:, step[1], OFF_V:OFF_V + VAL]]
                elif name == "out":
                    half, k = step[1]
                    out += [w_out_t[:, k, half * 512:half * 512 + 512]]
            return out

        STREAM = sources()
        assert len(STREAM) == BODY_UNITS

        @block.sync
        def _(sp):
            def load(n, src, before):
                if before is not None:
                    sp.wait_ge(w_lo_ok, before)
                dst = w_raw[:, n % STAGES, :]
                if len(src.shape) == 3:
                    dst = dst.rearrange("p (k e) -> p k e", e=P)
                sp.dma_start(dst, src).then_inc(w_ld[n % STAGES], 16)

            def load_ahead(b, i):
                n = i + SLOTS + STAGES
                if isinstance(b, int) and b == NB:
                    if n >= OUT_UNITS:
                        return
                    src = STREAM[FRONT_UNITS + n]
                else:
                    end = FRONT_UNITS if first(b) else BODY_UNITS
                    if n < end:
                        src = STREAM[n]
                    elif isinstance(b, int) and b == NB - 1:
                        src = STREAM[FRONT_UNITS + n - end]
                    else:
                        src = STREAM[n - end]
                load(n, src, base(b) + n - STAGES + 1)

            def x_load(b, t):
                if not (first(b) and t < 2):
                    sp.wait_ge(xt_pe, b * 2 * TT + 2 * (t - 1))
                if isinstance(b, int):
                    src = x_t[:, b * TT + t, :]
                else:
                    src = x_t[:, bass.ds(b * TT + t, 1), :].rearrange("p a d -> p (a d)")
                sp.dma_start(x_nat[:, t % 2, :], src).then_inc(x_ld[t % 2], 16)

            def tok(ap, b, half):
                if isinstance(b, int):
                    return ap[:, b * TT:b * TT + TT, half * 512:half * 512 + 512]
                return ap[:, bass.ds(b * TT, TT), half * 512:half * 512 + 512]

            def res_load(b, half):
                if half == 0:
                    sp.wait_ge(gn_lo, (b + 1) * HEADS)
                else:
                    sp.wait_ge(h_st, (b * 2 + 2) * 16)
                sp.dma_start(res[:, :, :], tok(x_t, b, half)).then_inc(res_ld, 16)

            def h_store(b, half):
                sp.wait_ge(low_sum_ok, sum_n(b + 1, half, TT - 1))
                sp.dma_start(tok(h_t, b, half), res[:, :, :]).then_inc(h_st, 16)

            for t in range(2):
                x_load(0, t)
            sp.dma_start(g1_row[:, :], norm1_g.partition_broadcast(P)).then_inc(consts_ld, 16)
            sp.dma_start(wz_raw[:, :, :], w_in_t[:, :, OFF_A:OFF_A + RANK]).then_inc(consts_ld, 16)
            for r in range(2):
                sp.dma_start(w_up[r * RANK:(r + 1) * RANK, :], w_gate_up).then_inc(consts_ld, 16)
            for dst, src in ((bg_col, b_gate), (cb_col, conv_b), (cg_col, conv_norm_g), (cnb_col, conv_norm_b)):
                sp.dma_start(dst[:, :], src).then_inc(consts_ld, 16)
            sp.dma_start(gn_col[:, :], gla_norm_g).then_inc(h_st, 16)
            sp.dma_start(cw_col[:, :, :], conv_w).then_inc(consts_ld, 16)

            def do(step, b):
                name = step[0]
                if name in ("conv_gate", "conv_in", "qk", "g", "v", "out"):
                    for i in range(step[3]):
                        load_ahead(b, step[2] + i)
                elif name == "x_prep":
                    x_load(b + 1, step[1])
                elif name == "out_done":
                    if step[1] == 0:
                        res_load(b - 1, 0)
                        h_store(b - 1, 0)
                        res_load(b - 1, 1)
                    else:
                        h_store(b - 1, 1)

            for n in range(STAGES):
                load(n, STREAM[n], None)
            for t in range(2, TT):
                x_load(0, t)
            for n in range(STAGES, STAGES + SLOTS):
                load(n, STREAM[n], n - STAGES + 1)
            run(sp, do)
            sp.wait_ge(h_st, (NB * 2 + 1) * 16)

        @block.gpsimd
        def _(pool):
            n_made = [0]

            def mk(ins):
                n_made[0] += 1
                ins.then_inc(made, 1)

            mk(nc.gpsimd.memset(neg_half[:, :], -0.5))
            mk(nc.gpsimd.memset(eps_col[:, :], EPS))
            mk(nc.gpsimd.memset(inv_d[:, :], 1.0 / D_MODEL))
            mk(nc.gpsimd.memset(one_col[:, :], 1.0))
            mk(nc.gpsimd.memset(ident[:, :], 0.0))
            mk(nc.gpsimd.memset(mean_dv[:, :], 1.0 / DV))
            mk(nc.gpsimd.memset(mean_grp[:, :], 0.0))
            mk(nc.gpsimd.memset(lvl_mask[:, :, :], 1.0))
            mk(nc.gpsimd.memset(ke[:, :, :, :], 0.0))
            mk(nc.gpsimd.memset(probs[:, :, :], 0.0))
            mk(nc.gpsimd.memset(state[:, :, :], 0.0))
            mk(nc.gpsimd.memset(u_sb[:, :, BLK:BLK + HALO], 0.0))
            pool.wait_ge(made, n_made[0])
            for g in range(P // CONV_GROUP):
                r = slice(g * CONV_GROUP, (g + 1) * CONV_GROUP)
                mk(nc.gpsimd.memset(mean_grp[r, r], 1.0 / CONV_GROUP))
                pool.wait_ge(made, n_made[0])
            mk(nc.gpsimd.affine_select(out=ident[:, :], in_=ident[:, :], compare_op=ALU.not_equal, fill=1.0,
                                       base=0, pattern=[[-1, P]], channel_multiplier=1))
            for lv, s in enumerate(LEVELS):
                m = lvl_mask[:, lv, :].rearrange("p (n s) -> p n s", s=s)
                n = P // (2 * s)
                mk(nc.gpsimd.affine_select(out=m, in_=m, compare_op=ALU.is_ge, fill=0.0, base=0,
                                           pattern=[[-2 * s, n], [0, s]], channel_multiplier=1))
            pool.wait_ge(made, n_made[0])
            for lv, s in enumerate(LEVELS):
                m = lvl_mask[:, lv, :].rearrange("p (n s) -> p n s", s=s)
                n = P // (2 * s)
                mk(nc.gpsimd.affine_select(out=m, in_=m, compare_op=ALU.is_ge, fill=0.0, base=s - 1,
                                           pattern=[[2 * s, n], [0, s]], channel_multiplier=-1))
            assert n_made[0] == MADE

            def split_lo(g, slot, stage):
                pool.wait_ge(w_hi_ok, g + 1)
                nc.gpsimd.tensor_tensor(w_lo[:, slot, :], w_raw[:, stage, :], w_hi[:, slot, :].bitcast(F32),
                                        ALU.subtract).then_inc(w_lo_ok, 1)

            def split_next(b, i):
                n = i + SLOTS
                if isinstance(b, int) and base(b) + n >= LAST_UNIT:
                    return
                split_lo(base(b) + n, n % SLOTS, n % STAGES)

            def x_rs(b, t):
                pool.wait_ge(x_ssq, b * TT + t + 1)
                for i, (a, const, op) in enumerate(((ssq, inv_d, ALU.mult), (rstd, eps_col, ALU.add),
                                                    (rstd, neg_half, ALU.pow))):
                    if i > 0:
                        pool.wait_ge(x_rstd, (b * TT + t) * 3 + i)
                    nc.gpsimd.tensor_tensor(rstd[:, t:t + 1], a[:, t:t + 1], const[:, :], op).then_inc(x_rstd, 1)

            def do(step, b):
                name = step[0]
                if name in ("conv_gate", "conv_in", "qk", "g", "v", "out"):
                    for i in range(step[3]):
                        split_next(b, step[2] + i)
                elif name == "x_prep":
                    x_rs(b + 1, step[1])
                elif name == "gla_factors":
                    c, m = step[1], b - 1
                    t = slice(c * P, (c + 1) * P)
                    pool.wait_ge(fac_ok, m * TT + c + 1)
                    if c == 0:
                        pool.wait_ge(qk_ok, m * 4 + 4)
                    if c > 0:
                        pool.wait_ge(kT_pe, m * TT + c)
                    if c > 1:
                        pool.wait_ge(o_pe, m * TT + c - 1)
                    nc.gpsimd.tensor_tensor(k_end[:, :, :], k_sb[:, :, t], fac[:, NL, :, :], ALU.mult)
                    nc.gpsimd.tensor_tensor(q_in[:, c % 2, :, :], q_sb[:, :, t], fac[:, NL + 1, :, :], ALU.mult)
                    nc.gpsimd.tensor_tensor(qk[:, :, :], q_sb[:, :, t], k_sb[:, :, t], ALU.mult)
                    for lv, s in enumerate(LEVELS):
                        f4 = fac[:, lv, :, :].rearrange("p a (n h s) -> p a n h s", h=2, s=s)
                        k4 = k_sb[:, :, t].rearrange("p a (n h s) -> p a n h s", h=2, s=s)
                        q4 = q_sb[:, :, t].rearrange("p a (n h s) -> p a n h s", h=2, s=s)
                        o4 = ke[:, lv, :, :].rearrange("p a (n h s) -> p a n h s", h=2, s=s)
                        nc.gpsimd.tensor_tensor(o4[:, :, :, 0, :], k4[:, :, :, 0, :], f4[:, :, :, 0, :], ALU.mult)
                        ins = nc.gpsimd.tensor_tensor(qe[:, lv, :, :].rearrange("p a (n s) -> p a n s", s=s),
                                                      q4[:, :, :, 1, :], f4[:, :, :, 1, :], ALU.mult)
                    ins.then_inc(ke_ok, 1)
                elif name == "cn_rstd":
                    m = b - 1
                    for j in range(CT):
                        pool.wait_ge(cn_rs, (m * CT + j) * 2 + 2)
                        nc.gpsimd.tensor_tensor(y_sb[:, j, :], y_sb[:, j, :], nr[:, j, :], ALU.mult).then_inc(cn_n, 1)
                elif name == "cn_mixed":
                    m = b - 1
                    for j in range(CT):
                        pool.wait_ge(cn_sig, m * CT + j + 1)
                        pool.wait_ge(cn_aff, m * CT + j + 1)
                        nc.gpsimd.tensor_tensor(y_sb[:, j, :], y_sb[:, j, :], nr[:, j, :], ALU.mult).then_inc(cn_f, 1)
                        pool.wait_ge(cn_hi, m * CT + j + 1)
                        nc.gpsimd.tensor_tensor(mix_lo[:, HEADS + j, :], y_sb[:, j, :],
                                                mix_hi[:, HEADS + j, :].bitcast(F32), ALU.subtract).then_inc(cn_lo, 1)
                elif name == "gn_mixed":
                    m = b - 1
                    for h in range(HEADS):
                        pool.wait_ge(gn_n, m * HEADS + h + 1)
                        nc.gpsimd.tensor_tensor(o_sb[:, h, :], o_sb[:, h, :], silu_g[:, h, :], ALU.mult).then_inc(gn_f, 1)
                        pool.wait_ge(gn_hi, m * HEADS + h + 1)
                        nc.gpsimd.tensor_tensor(mix_lo[:, h, :], o_sb[:, h, :],
                                                mix_hi[:, h, :].bitcast(F32), ALU.subtract).then_inc(gn_lo, 1)

            for t in range(TT):
                x_rs(0, t)
            for g in range(SLOTS):
                split_lo(g, g, g)
            run(pool, do)

        @block.scalar
        def _(act):
            act.wait_ge(made, MADE)

            def split_hi(g, slot, stage, b, n):
                act.wait_ge(w_ld[stage], (stage_round(b, n) + 1) * 16)
                if not (first(b) and n < SLOTS):
                    act.wait_ge(w_used, g - SLOTS + 1)
                nc.scalar.activation(w_hi[:, slot, :], w_raw[:, stage, :], ACT.Copy).then_inc(w_hi_ok, 1)

            def stage_round(b, n):
                if first(b):
                    return n // STAGES
                return b * (BODY_UNITS // STAGES) - OUT_UNITS // STAGES + n // STAGES

            def split_next(b, i):
                n = i + SLOTS
                if isinstance(b, int) and base(b) + n >= LAST_UNIT:
                    return
                split_hi(base(b) + n, n % SLOTS, n % STAGES, b, n)

            def x_sq(b, t):
                act.wait_ge(x_ld[t % 2], (b * 2 + t // 2 + 1) * 16)
                if not (first(b) and t == 0):
                    act.wait_ge(x_ssq, b * TT + t)
                if not first(b):
                    act.wait_ge(x_norm, (b - 1) * TT + t + 1)
                nc.scalar.activation(junk[:, :], x_nat[:, t % 2, :], ACT.Square,
                                     accum_out=ssq[:, t:t + 1]).then_inc(x_ssq, 1)

            def xt_hi(b, t):
                for g in range(2):
                    act.wait_ge(xt_pe, b * 2 * TT + 2 * t + g + 1)
                    src = acc[:, X_BANKS[t][g], :].rearrange("p (k c) -> p k c", c=P)
                    nc.scalar.activation(xT_hi[:, g * 4:g * 4 + 4, t * P:(t + 1) * P], src,
                                         ACT.Copy).then_inc(xt_hi_ok, 1)

            def do(step, b):
                name = step[0]
                if name in ("conv_gate", "conv_in", "qk", "g", "v", "out"):
                    for i in range(step[3]):
                        split_next(b, step[2] + i)
                if name == "conv_gate":
                    j = step[1]
                    act.wait_ge(w_used, base(b) + step[2] + 2)
                    if j >= 2:
                        act.wait_ge(u_ok, b * 2 * CT + 2 * (j - 1))
                    elif not first(b):
                        act.wait_ge(silu_ok, b * HEADS - 1 + j - 1 + 1)
                    nc.scalar.activation(sig[:, j % 2, :], acc[:, 0, :], ACT.Sigmoid).then_inc(csig_ok, 1)
                elif name == "z":
                    act.wait_ge(z_pe, b + 1)
                    if not first(b):
                        act.wait_ge(gate_pe, b * PAIRS)
                    nc.scalar.activation(z_sb[:, :], acc[0:2 * RANK, 0, :], ACT.Copy).then_inc(z_ok, 1)
                elif name == "gate":
                    j = step[1]
                    act.wait_ge(gate_pe, b * PAIRS + j + 1)
                    if j == 0:
                        act.wait_ge(u_ok, (b + 1) * 2 * CT)
                    nc.scalar.activation(log1p_t[:, j, :], acc[:, 0, :], ACT.Abs,
                                         bias=bg_col[:, j:j + 1]).then_inc(gate_act, 1)
                elif name == "decay":
                    act.wait_ge(gate_act, b * 4 + 2)
                    nc.scalar.activation(log1p_t[:, :, :], log1p_t[:, :, :], ACT.Exp, scale=-1.0).then_inc(gate_act, 1)
                    act.wait_ge(gate_act, b * 4 + 3)
                    nc.scalar.activation(log1p_t[:, :, :], log1p_t[:, :, :], ACT.Ln,
                                         bias=one_col[:, :]).then_inc(gate_act, 1)
                elif name == "qk":
                    j = step[1]
                    act.wait_ge(w_used, base(b) + step[2] + 2)
                    if j == 0 and not first(b):
                        act.wait_ge(ke_ok, b * TT)
                    dst = (q_sb if j < PAIRS else k_sb)[:, j % PAIRS, :]
                    nc.scalar.activation(dst, acc[:, QK_BANK[j], :], ACT.Copy,
                                         scale=DK ** -0.5 if j < PAIRS else 1.0).then_inc(qk_ok, 1)
                elif name == "v_done":
                    act.wait_ge(w_used, base(b) + step[1] + 1)
                    if not first(b):
                        act.wait_ge(upd_pe, b * TT)
                    for t in range(TT):
                        nc.scalar.activation(v_sb[:, t, :], acc[:, 2 + t, :], ACT.Copy).then_inc(v_ok, 1)
                elif name == "g":
                    j = step[1]
                    act.wait_ge(w_used, base(b) + step[2] + 2)
                    if j >= 2:
                        act.wait_ge(silu_ok, b * HEADS + j - 1)
                    else:
                        act.wait_ge(cum_ok, (b + 1) * PAIRS * TT)
                    nc.scalar.activation(sig[:, j % 2, :], acc[:, G_BANK[j], :], ACT.Sigmoid).then_inc(gsig_ok, 1)
                elif name == "x_prep":
                    x_sq(b + 1, step[1])
                    xt_hi(b + 1, step[1])
                elif name == "gla_factors":
                    c, m = step[1], b - 1
                    act.wait_ge(expo_ok, m * TT + c + 1)
                    if c > 1:
                        act.wait_ge(state_ok, (m * TT + c - 1) * HEADS)
                    nc.scalar.activation(decay[:, c % 2, :], cum[:, :, (c + 1) * P - 1], ACT.Exp, scale=1.0 / TAU)
                    nc.scalar.activation(fac[:, 0:NL + 1, :, :], fac[:, 0:NL + 1, :, :], ACT.Exp, scale=1.0 / TAU)
                    nc.scalar.activation(fac[:, NL + 1, :, :], cum[:, :, c * P:(c + 1) * P], ACT.Exp,
                                         scale=1.0 / TAU).then_inc(fac_ok, 1)
                elif name == "gla_select":
                    c, m = step[1], b - 1
                    act.wait_ge(kT_pe, m * TT + c + 1)
                    if c > 0:
                        act.wait_ge(upd_pe, m * TT + c)
                    nc.scalar.activation(k_endT[:, :, :], acc[:, 7, 0:KEY].rearrange("p (a c) -> p a c", c=P),
                                         ACT.Copy).then_inc(kT_ok, 1)
                elif name == "gla_out":
                    c, m = step[1], b - 1
                    act.wait_ge(o_pe, m * TT + c + 1)
                    if c == 0:
                        act.wait_ge(h_st, (m * 2 + 1) * 16)
                    nc.scalar.activation(o_sb[:, :, c * P:(c + 1) * P], acc[:, 6, :].rearrange("p (h c) -> p h c", c=P),
                                         ACT.Copy).then_inc(o_ok, 1)
                elif name == "cn_mean":
                    m = b - 1
                    for j in range(CT):
                        act.wait_ge(cn_dev, m * CT + j + 1)
                        nc.scalar.activation(nr[:, j, :], y_sb[:, j, :], ACT.Square).then_inc(cn_sq, 1)
                elif name == "cn_rstd":
                    m = b - 1
                    for j in range(CT):
                        act.wait_ge(cn_var_pe, m * CT + j + 1)
                        nc.scalar.activation(nr[:, j, :], acc[:, 2 + j, :], ACT.Ln, bias=eps_col[:, :]).then_inc(cn_rs, 1)
                        act.wait_ge(cn_rs, (m * CT + j) * 2 + 1)
                        nc.scalar.activation(nr[:, j, :], nr[:, j, :], ACT.Exp, scale=-0.5).then_inc(cn_rs, 1)
                elif name == "cn_mixed":
                    m = b - 1
                    for j in range(CT):
                        act.wait_ge(cn_n, m * CT + j + 1)
                        nc.scalar.activation(nr[:, j, :], y_sb[:, j, :], ACT.Sigmoid, bias=cnb_col[:, j:j + 1],
                                             scale=cg_col[:, j:j + 1]).then_inc(cn_sig, 1)
                    for j in range(CT):
                        act.wait_ge(cn_f, m * CT + j + 1)
                        nc.scalar.activation(mix_hi[:, HEADS + j, :], y_sb[:, j, :], ACT.Copy).then_inc(cn_hi, 1)
                elif name == "gn_square":
                    m = b - 1
                    act.wait_ge(o_ok, (m + 1) * TT)
                    act.wait_ge(cn_f, (m + 1) * CT)
                    for h in range(HEADS):
                        nc.scalar.activation(nr[:, h, :], o_sb[:, h, :], ACT.Square).then_inc(gn_sq, 1)
                elif name == "gn_rstd":
                    m = b - 1
                    for h in range(HEADS):
                        act.wait_ge(gn_sum_pe, m * HEADS + h + 1)
                        nc.scalar.activation(nr[:, h, :], acc[:, 2 + h, :], ACT.Ln, bias=eps_col[:, :]).then_inc(gn_rs, 1)
                        act.wait_ge(gn_rs, (m * HEADS + h) * 2 + 1)
                        nc.scalar.activation(nr[:, h, :], nr[:, h, :], ACT.Exp, scale=-0.5).then_inc(gn_rs, 1)
                elif name == "gn_mixed":
                    m = b - 1
                    for h in range(HEADS):
                        act.wait_ge(gn_f, m * HEADS + h + 1)
                        nc.scalar.activation(mix_hi[:, h, :], o_sb[:, h, :], ACT.Copy).then_inc(gn_hi, 1)

            for t in range(TT):
                x_sq(0, t)
                xt_hi(0, t)
            act.wait_ge(consts_ld, CONSTS)
            nc.scalar.activation(wz[:, :, 0, :], wz_raw[:, :, :], ACT.Copy).then_inc(wz_ok, 1)
            for g in range(SLOTS):
                split_hi(g, g, g, 0, g)
            run(act, do)

        @block.vector
        def _(dve):
            dve.wait_ge(made, MADE)
            dve.wait_ge(consts_ld, CONSTS)
            dve.wait_ge(h_st, 16)

            def carry_wait():
                nc.vector.tensor_copy(pace[:, :], one_col[:, :])

            def x_nrm(b, t):
                dve.wait_ge(x_rstd, (b * TT + t + 1) * 3)
                nc.vector.scalar_tensor_tensor(out=x_nat[:, t % 2, :], in0=x_nat[:, t % 2, :],
                                               scalar=rstd[:, t:t + 1], in1=g1_row[:, :],
                                               op0=ALU.mult, op1=ALU.mult).then_inc(x_norm, 1)
                for g in range(2):
                    dve.wait_ge(xt_hi_ok, b * 2 * TT + 2 * t + g + 1)
                    src = acc[:, X_BANKS[t][g], :].rearrange("p (k c) -> p k c", c=P)
                    at = (slice(None), slice(g * 4, g * 4 + 4), slice(t * P, (t + 1) * P))
                    nc.vector.tensor_tensor(xT_lo[at], src, xT_hi[at].bitcast(F32), ALU.subtract).then_inc(low_sum_ok, 1)

            def do(step, b):
                name = step[0]
                if name == "conv_in":
                    j = step[1]
                    if j == 0 and not first(b):
                        dve.wait_ge(tap_ok, b * TAPS * CT)
                    nc.vector.tensor_copy(u_sb[:, j, 0:HALO], u_sb[:, j, BLK:BLK + HALO]).then_inc(u_ok, 1)
                    dve.wait_ge(w_used, base(b) + step[2] + 2)
                    dve.wait_ge(csig_ok, b * CT + j + 1)
                    dve.wait_ge(u_ok, b * 2 * CT + 2 * j + 1)
                    nc.vector.tensor_tensor(u_sb[:, j, HALO:HALO + BLK], acc[:, 1, :], sig[:, j % 2, :],
                                            ALU.mult).then_inc(u_ok, 1)
                elif name == "taps":
                    k = step[1]
                    for j in range(CT):
                        if k == 0:
                            if j == 0:
                                dve.wait_ge(u_ok, (b + 1) * 2 * CT)
                                if not first(b):
                                    dve.wait_ge(cn_lo, b * CT)
                            nc.vector.tensor_scalar(y_sb[:, j, :], u_sb[:, j, 0:BLK], cw_col[:, j, 0:1],
                                                    cb_col[:, j:j + 1], ALU.mult, ALU.add).then_inc(tap_ok, 1)
                        else:
                            dve.wait_ge(tap_ok, b * TAPS * CT + (k - 1) * CT + j + 1)
                            nc.vector.scalar_tensor_tensor(out=y_sb[:, j, :], in0=u_sb[:, j, k:k + BLK],
                                                           scalar=cw_col[:, j, k:k + 1], in1=y_sb[:, j, :],
                                                           op0=ALU.mult, op1=ALU.add).then_inc(tap_ok, 1)
                elif name == "gate":
                    j = step[1]
                    dve.wait_ge(gate_act, b * 4 + j + 1)
                    if j == 0 and not first(b):
                        dve.wait_ge(fac_ok, b * TT)
                    nc.vector.tensor_scalar(cum[:, j, :], acc[:, 0, :], bg_col[:, j:j + 1], 0.0,
                                            ALU.add, ALU.min).then_inc(gate_min, 1)
                elif name == "decay":
                    dve.wait_ge(gate_act, b * 4 + 4)
                    dve.wait_ge(gate_min, (b + 1) * PAIRS)
                    for j in range(PAIRS):
                        for c in range(TT):
                            t = slice(c * P, (c + 1) * P)
                            nc.vector.tensor_tensor_scan(cum[:, j, t], cum[:, j, t], log1p_t[:, j, t], 0.0,
                                                         ALU.add, ALU.subtract).then_inc(cum_ok, 1)
                elif name == "g":
                    j = step[1]
                    dve.wait_ge(gsig_ok, b * HEADS + j + 1)
                    if j == 0 and not first(b):
                        dve.wait_ge(gn_f, b * HEADS)
                    nc.vector.tensor_tensor(silu_g[:, j, :], acc[:, G_BANK[j], :], sig[:, j % 2, :],
                                            ALU.mult).then_inc(silu_ok, 1)
                elif name == "x_prep":
                    x_nrm(b + 1, step[1])
                elif name == "out_done":
                    half, m = step[1], b - 1
                    dve.wait_ge(res_ld, (m * 2 + half + 1) * 16)
                    for t in range(TT):
                        if t < TT - 1:
                            dve.wait_ge(out_pe, (m * 2 + half) * (TT - 1) + t + 1)
                        else:
                            dve.wait_ge(w_used, base(b) + step[2] + 1)
                        nc.vector.tensor_tensor(res[:, t, :], acc[:, OUT_BANKS[half][t], :], res[:, t, :],
                                                ALU.add).then_inc(low_sum_ok, 1)
                elif name == "gla_factors":
                    c, m = step[1], b - 1
                    if c == 0:
                        dve.wait_ge(cum_ok, (m + 1) * 2 * TT)
                    if c > 0:
                        dve.wait_ge(ke_ok, m * TT + c)
                    cc = cum[:, :, c * P:(c + 1) * P]
                    for lv, s in enumerate(LEVELS):
                        n = P // (2 * s)
                        c5 = cc.rearrange("p a (n h s) -> p a n h s", h=2, s=s)
                        f5 = fac[:, lv, :, :].rearrange("p a (n h s) -> p a n h s", h=2, s=s)
                        ref = c5[:, :, :, 0, s - 1:s].broadcast_to([P, PAIRS, n, s])
                        nc.vector.tensor_tensor(f5[:, :, :, 0, :], ref, c5[:, :, :, 0, :], ALU.subtract)
                        nc.vector.tensor_tensor(f5[:, :, :, 1, :], c5[:, :, :, 1, :], ref, ALU.subtract)
                    nc.vector.tensor_tensor(fac[:, NL, :, :], cc[:, :, P - 1:P].broadcast_to([P, PAIRS, P]), cc,
                                            ALU.subtract).then_inc(expo_ok, 1)
                elif name == "gla_select":
                    c, m = step[1], b - 1
                    dve.wait_ge(score_pe, m * TT + c + 1)
                    if c > 0:
                        dve.wait_ge(o_pe, m * TT + c)
                    n0 = (m * TT + c) * (NL + 1)
                    carry_wait()
                    diag = acc[:, 2:2 + HEADS, NL * 64:NL * 64 + 1].broadcast_to([P, HEADS, P])
                    nc.vector.copy_predicated(probs[:, :, :], ident[:, :].bitcast(I32).unsqueeze(1).broadcast_to([P, HEADS, P]),
                                              diag).then_inc(probs_ok, 1)
                    for lv, s in enumerate(LEVELS):
                        n = P // (2 * s)
                        dve.wait_ge(probs_ok, n0 + lv + 1)
                        carry_wait()
                        dst = probs[:, :, :].rearrange("p a (n h s) -> p a n h s", h=2, s=s)[:, :, :, 1, :]
                        src = acc[:, 2:2 + HEADS, lv * 64:lv * 64 + 64].rearrange("p a (n s) -> p a n s", s=s)
                        msk = lvl_mask[:, lv, :].bitcast(I32).rearrange("p (n s) -> p n s", s=s)
                        nc.vector.copy_predicated(dst, msk.unsqueeze(1).broadcast_to([P, HEADS, n, s]),
                                                  src).then_inc(probs_ok, 1)
                elif name == "gla_out":
                    c, m = step[1], b - 1
                    dve.wait_ge(upd_pe, m * TT + c + 1)
                    if c > 0:
                        dve.wait_ge(state_ok, (m * TT + c) * HEADS)
                    for h in range(HEADS):
                        a, r = h // 2, slice(h % 2 * DK, h % 2 * DK + DK)
                        nc.vector.scalar_tensor_tensor(out=state[r, h, :], in0=state[r, h, :],
                                                       scalar=decay[r, c % 2, a:a + 1],
                                                       in1=acc[r, 7, KEY + a * DV:KEY + (a + 1) * DV],
                                                       op0=ALU.mult, op1=ALU.add).then_inc(state_ok, 1)
                elif name == "cn_mean":
                    m = b - 1
                    for j in range(CT):
                        dve.wait_ge(cn_mean_pe, m * CT + j + 1)
                        nc.vector.tensor_tensor(y_sb[:, j, :], y_sb[:, j, :], acc[:, 2 + j, :],
                                                ALU.subtract).then_inc(cn_dev, 1)
                elif name == "cn_mixed":
                    m = b - 1
                    for j in range(CT):
                        dve.wait_ge(cn_sig, m * CT + j + 1)
                        nc.vector.tensor_scalar(y_sb[:, j, :], y_sb[:, j, :], cg_col[:, j:j + 1], cnb_col[:, j:j + 1],
                                                ALU.mult, ALU.add).then_inc(cn_aff, 1)
                elif name == "gn_mixed":
                    m = b - 1
                    for h in range(HEADS):
                        dve.wait_ge(gn_rs, (m * HEADS + h) * 2 + 2)
                        nc.vector.scalar_tensor_tensor(out=o_sb[:, h, :], in0=o_sb[:, h, :], scalar=gn_col[:, 0:1],
                                                       in1=nr[:, h, :], op0=ALU.mult, op1=ALU.mult).then_inc(gn_n, 1)

            for t in range(TT):
                x_nrm(0, t)
            dve.wait_ge(wz_ok, 1)
            nc.vector.tensor_tensor(wz[:, :, 1, :], wz_raw[:, :, :], wz[:, :, 0, :].bitcast(F32),
                                    ALU.subtract).then_inc(wz_ok, 1)
            run(dve, do)

        @block.tensor
        def _(pe):
            pe.wait_ge(made, MADE)
            pe.wait_ge(consts_ld, CONSTS)

            def x_tr(b, t):
                pe.wait_ge(x_norm, b * TT + t + 1)
                for g in range(2):
                    bank = X_BANKS[t][g]
                    free_bank_x(b, t, g)
                    for k in range(4):
                        kk = g * 4 + k
                        ins = nc.tensor.transpose(acc[:, bank, k * P:(k + 1) * P],
                                                  x_nat[:, t % 2, kk * P:(kk + 1) * P], ident[:, :])
                    ins.then_inc(xt_pe, 1)

            def free_bank_x(b, t, g):
                if first(b):
                    return
                m = b - 1
                if t == 0:
                    pe.wait_ge(silu_ok, m * HEADS + 4)
                elif t == 1:
                    if not first(m):
                        pe.wait_ge(o_ok, m * TT)
                        pe.wait_ge(state_ok, m * TT * HEADS)
                elif not first(m):
                    pe.wait_ge(low_sum_ok, sum_n(m, 0, TT - 1))
                else:
                    pe.wait_ge(v_ok, (m + 1) * TT)

            def weights(b, i):
                pe.wait_ge(w_lo_ok, base(b) + i + 1)

            def column_tile(step, b, bank):
                for i in range(2):
                    n = step[2] + i
                    weights(b, n)
                    for k in range(4):
                        kk = i * 4 + k
                        c = slice(k * P, (k + 1) * P)
                        ins = three_products(nc, acc[:, bank, :], w_hi[:, n % SLOTS, c], w_lo[:, n % SLOTS, c],
                                             xT_hi[:, kk, :], xT_lo[:, kk, :], kk == 0, kk == KT - 1)
                    ins.then_inc(w_used, 1)

            def do(step, b):
                name = step[0]
                if name == "conv_gate":
                    j = step[1]
                    if j == 0:
                        pe.wait_ge(low_sum_ok, low_sum_start(b))
                        if not first(b):
                            if isinstance(b, int) or True:
                                wait_out1(b)
                    else:
                        pe.wait_ge(csig_ok, b * CT + j)
                    column_tile(step, b, 0)
                elif name == "conv_in":
                    j = step[1]
                    if j > 0:
                        pe.wait_ge(u_ok, b * 2 * CT + 2 * j)
                    column_tile(step, b, 1)
                elif name == "z":
                    pe.wait_ge(csig_ok, (b + 1) * CT)
                    if first(b):
                        pe.wait_ge(wz_ok, 2)
                    for k in range(KT):
                        w = wz[:, k, :, :].rearrange("p a r -> p (a r)")
                        nc.tensor.matmul(acc[0:2 * RANK, 0, :], w, xT_hi[:, k, :], start=(k == 0), stop=False)
                        ins = nc.tensor.matmul(acc[0:2 * RANK, 0, :], w, xT_lo[:, k, :], start=False, stop=(k == KT - 1))
                    ins.then_inc(z_pe, 1)
                elif name == "gate":
                    j = step[1]
                    if j == 0:
                        pe.wait_ge(z_ok, b + 1)
                    else:
                        pe.wait_ge(gate_min, b * PAIRS + j)
                    nc.tensor.matmul(acc[:, 0, :], w_up[:, j * P:(j + 1) * P], z_sb[:, :], start=True,
                                     stop=True).then_inc(gate_pe, 1)
                elif name == "qk":
                    j = step[1]
                    if j == 0:
                        pe.wait_ge(u_ok, (b + 1) * 2 * CT)
                    elif j < 3:
                        pe.wait_ge(qk_ok, b * 4 + j)
                    else:
                        pe.wait_ge(gate_min, (b + 1) * PAIRS)
                    column_tile(step, b, QK_BANK[j])
                elif name == "v":
                    k = step[1]
                    if k == 0 and not first(b):
                        pe.wait_ge(gn_rs, b * HEADS * 2)
                    weights(b, step[2])
                    slot = step[2] % SLOTS
                    for t in range(TT):
                        c = slice(t * P, (t + 1) * P)
                        out = acc[:, 2 + t, :]
                        nc.tensor.matmul(out, xT_hi[:, k, c], w_hi[:, slot, :], start=(k == 0), stop=False)
                        nc.tensor.matmul(out, xT_hi[:, k, c], w_lo[:, slot, :], start=False, stop=False)
                        ins = nc.tensor.matmul(out, xT_lo[:, k, c], w_hi[:, slot, :], start=False, stop=(k == KT - 1))
                    ins.then_inc(w_used, 1)
                elif name == "g":
                    j = step[1]
                    if j == 0:
                        pe.wait_ge(qk_ok, b * 4 + 3)
                    elif j == 1:
                        pe.wait_ge(qk_ok, b * 4 + 4)
                    else:
                        pe.wait_ge(silu_ok, b * HEADS + j - 1)
                    column_tile(step, b, G_BANK[j])
                elif name == "x_prep":
                    x_tr(b + 1, step[1])
                elif name == "out":
                    (half, k), m = step[1], b - 1
                    if k == 0:
                        if half == 0:
                            if isinstance(b, int) and b == NB:
                                pe.wait_ge(gn_rs, b * HEADS * 2)
                            else:
                                pe.wait_ge(v_ok, (b + 1) * TT)
                            pe.wait_ge(cn_lo, b * CT)
                            pe.wait_ge(gn_lo, b * HEADS)
                        else:
                            pe.wait_ge(o_ok, b * TT)
                            pe.wait_ge(state_ok, b * TT * HEADS)
                            if not (isinstance(b, int) and b >= NB - 1):
                                pe.wait_ge(low_sum_ok, low_n(b, 1))
                            if isinstance(b, int) and b == NB - 1:
                                pe.wait_ge(silu_ok, (b + 1) * HEADS)
                    weights(b, step[2])
                    slot = step[2] % SLOTS
                    for t in range(TT):
                        c = slice(t * P, (t + 1) * P)
                        out = acc[:, OUT_BANKS[half][t], :]
                        nc.tensor.matmul(out, mix_hi[:, k, c], w_hi[:, slot, :], start=(k == 0), stop=False)
                        nc.tensor.matmul(out, mix_hi[:, k, c], w_lo[:, slot, :], start=False, stop=False)
                        ins = nc.tensor.matmul(out, mix_lo[:, k, c], w_hi[:, slot, :], start=False, stop=(k == KT - 1))
                        if t == TT - 1:
                            ins.then_inc(w_used, 1)
                        elif k == KT - 1:
                            ins.then_inc(out_pe, 1)
                elif name == "cn_mean":
                    m = b - 1
                    pe.wait_ge(tap_ok, b * TAPS * CT)
                    if isinstance(b, int) and b == NB or True:
                        wait_stat_banks(b)
                    for j in range(CT):
                        nc.tensor.matmul(acc[:, 2 + j, :], mean_grp[:, :], y_sb[:, j, :], start=True,
                                         stop=True).then_inc(cn_mean_pe, 1)
                elif name == "cn_var":
                    m = b - 1
                    for j in range(CT):
                        pe.wait_ge(cn_sq, m * CT + j + 1)
                        nc.tensor.matmul(acc[:, 2 + j, :], mean_grp[:, :], nr[:, j, :], start=True,
                                         stop=True).then_inc(cn_var_pe, 1)
                elif name == "gla_scores":
                    c, m = step[1], b - 1
                    pe.wait_ge(ke_ok, m * TT + c + 1)
                    if c == 0:
                        pe.wait_ge(cn_rs, b * CT * 2)
                    else:
                        pe.wait_ge(probs_ok, (m * TT + c) * (NL + 1))
                    for h in range(HEADS):
                        a, r = h // 2, slice(h % 2 * DK, h % 2 * DK + DK)
                        for lv in range(NL):
                            nc.tensor.matmul(acc[:, 2 + h, lv * 64:lv * 64 + 64], ke[r, lv, a, :], qe[r, lv, a, :],
                                             start=True, stop=True)
                        ins = nc.tensor.matmul(acc[:, 2 + h, NL * 64:NL * 64 + 1], qk[r, a, :], one_col[r, :],
                                               start=True, stop=True)
                    ins.then_inc(score_pe, 1)
                    if c > 0:
                        pe.wait_ge(state_ok, (m * TT + c) * HEADS)
                    for a in range(PAIRS):
                        ins = nc.tensor.transpose(acc[:, 7, a * P:(a + 1) * P], k_end[:, a, :], ident[:, :])
                    ins.then_inc(kT_pe, 1)
                elif name == "gla_out":
                    c, m = step[1], b - 1
                    if c == 0:
                        pe.wait_ge(v_ok, b * TT)
                    else:
                        pe.wait_ge(o_ok, m * TT + c)
                    pe.wait_ge(probs_ok, (m * TT + c + 1) * (NL + 1))
                    for h in range(HEADS):
                        a = h // 2
                        out = acc[:, 6, h * P:(h + 1) * P]
                        nc.tensor.matmul(out, state[:, h, :], q_in[:, c % 2, a, :], start=True, stop=False)
                        ins = nc.tensor.matmul(out, v_sb[:, c, h * DV:(h + 1) * DV], probs[:, h, :],
                                               start=False, stop=True)
                    ins.then_inc(o_pe, 1)
                    pe.wait_ge(kT_ok, m * TT + c + 1)
                    for h in range(HEADS):
                        a, r = h // 2, slice(h % 2 * DK, h % 2 * DK + DK)
                        ins = nc.tensor.matmul(acc[r, 7, KEY + a * DV:KEY + (a + 1) * DV], k_endT[:, a, r],
                                               v_sb[:, c, h * DV:(h + 1) * DV], start=True, stop=True)
                    ins.then_inc(upd_pe, 1)
                elif name == "gn_sum":
                    m = b - 1
                    for h in range(HEADS):
                        pe.wait_ge(gn_sq, m * HEADS + h + 1)
                        nc.tensor.matmul(acc[:, 2 + h, :], mean_dv[:, :], nr[:, h, :], start=True,
                                         stop=True).then_inc(gn_sum_pe, 1)

            def wait_out1(b):
                pe.wait_ge(silu_ok, b * HEADS)

            def wait_stat_banks(b):
                pe.wait_ge(v_ok, b * TT)

            for t in range(TT):
                x_tr(0, t)
            run(pe, do)


CONSTS = 16 * (1 + 1 + 2 + 4 + 1)
MADE = 12 + P // CONV_GROUP + 1 + 2 * NL
QK_BANK = [1, 1, 1, 0]
G_BANK = [1, 0, 1, 0]
X_BANKS = [(0, 1), (6, 7), (2, 3), (4, 5)]
OUT_BANKS = [(2, 3, 4, 5), (0, 1, 6, 7)]


def mlp_block(nc, h_dram, norm2_g, w_mlp_in, w_mlp_out, final_norm_g, out):
    with ExitStack() as ctx:
        def sb(name, shape, dt=F32):
            return ctx.enter_context(nc.sbuf_tensor(name, shape, dt))

        def sem(name):
            return ctx.enter_context(nc.semaphore(name))

        h_sb = sb("h_sb", [P, HT, D_MODEL])
        hn = sb("hn", [P, 2, D_MODEL])
        m_junk = sb("m_junk", [P, D_MODEL], BF16)
        g2_row = sb("g2_row", [P, D_MODEL])
        gf_row = sb("gf_row", [P, D_MODEL])
        m_ssq = sb("m_ssq", [P, HT])
        m_rstd = sb("m_rstd", [P, HT])
        m_neg_half = sb("m_neg_half", [P, 1])
        m_eps = sb("m_eps", [P, 1])
        m_inv_d = sb("m_inv_d", [P, 1])
        m_ident = sb("m_ident", [P, P])
        hT_hi = sb("hT_hi", [P, KT, HALF], F32R)
        hT_lo = sb("hT_lo", [P, KT, HALF], F32R)
        raw = sb("raw", [P, 2 * FT, D_MODEL])
        m_hi = sb("m_hi", [P, 2 * FT, D_MODEL], F32R)
        m_lo = sb("m_lo", [P, 2 * FT, D_MODEL], F32R)
        relu = sb("relu", [P, 2 * FT, 512])
        ff_hi = sb("ff_hi", [P, FT, HALF], F32R)
        ff_lo = sb("ff_lo", [P, FT, HALF], F32R)
        ps = ctx.enter_context(nc.psum_tensor("ps", [P, 8, 512], F32))

        rows_ld = sem("rows_ld")
        m_made = sem("m_made")
        h_ld = sem("h_ld")
        sq_ok = sem("sq_ok")
        rs_ok = sem("rs_ok")
        hn_ok = sem("hn_ok")
        m_ld = [sem(f"m_ld{i}") for i in range(2 * FT)]
        m_hi_ok = sem("m_hi_ok")
        m_lo_ok = sem("m_lo_ok")
        up_pe = sem("up_pe")
        relu_ok = sem("relu_ok")
        sqr_ok = sem("sqr_ok")
        ff_hi_ok = sem("ff_hi_ok")
        ff_lo_ok = sem("ff_lo_ok")
        down_pe = sem("down_pe")
        add_ok = sem("add_ok")
        fsq_ok = sem("fsq_ok")
        frs_ok = sem("frs_ok")
        fin_ok = sem("fin_ok")
        out_st = sem("out_st")
        block = ctx.enter_context(nc.Block())

        NG = HT * 2
        NT = HT * 2

        def up_n(half, f):
            return f * 4 + (half + 1) * NT

        def add_n(half, f):
            return f * NG + (half + 1) * NT

        h_t = h_dram.rearrange("(n p) d -> p n d", p=P)
        out_t = out.rearrange("(n p) d -> p n d", p=P)
        w1_t = w_mlp_in.rearrange("(k p) f -> p k f", p=P)
        w2_t = w_mlp_out.rearrange("(f p) d -> p f d", p=P)

        @block.sync
        def _(sp):
            sp.dma_start(g2_row[:, :], norm2_g.partition_broadcast(P)).then_inc(rows_ld, 16)
            sp.dma_start(gf_row[:, :], final_norm_g.partition_broadcast(P)).then_inc(rows_ld, 16)
            for half in range(NH):
                for t in range(HT):
                    if half > 0:
                        sp.wait_ge(out_st, (t + 1) * 16)
                    if t < 1:
                        pass
                    sp.dma_start(h_sb[:, t, :], h_t[:, half * HT + t, :]).then_inc(h_ld, 16)
                    sp.wait_ge(h_ld, (half * HT + t + 1) * 16)
                def step_weights(f):
                    for i in range(2 * FT):
                        if half > 0 or not isinstance(f, int):
                            sp.wait_ge(m_lo_ok, (f + half * NF - 1) * 2 * FT + i + 1)
                        if i < FT:
                            src = w1_t[:, :, bass.ds(f * FC + i * P, P)]
                            dst = raw[:, i, :].rearrange("p (k c) -> p k c", c=P)
                        else:
                            src = w2_t[:, bass.ds(f * FT + i - FT, 1), :].rearrange("p a d -> p (a d)")
                            dst = raw[:, i, :]
                        sp.dma_start(dst, src).then_inc(m_ld[i], 16)

                step_weights(0)
                with sp.Fori(1, NF) as f:
                    step_weights(f)
                for t in range(HT):
                    sp.wait_ge(fin_ok, half * HT + t + 1)
                    sp.dma_start(out_t[:, half * HT + t, :], h_sb[:, t, :]).then_inc(out_st, 16)
                    sp.wait_ge(out_st, (half * HT + t + 1) * 16)

        @block.gpsimd
        def _(pool):
            nc.gpsimd.memset(m_neg_half[:, :], -0.5)
            nc.gpsimd.memset(m_eps[:, :], EPS)
            nc.gpsimd.memset(m_inv_d[:, :], 1.0 / D_MODEL)
            nc.gpsimd.memset(m_ident[:, :], 0.0).then_inc(m_made, 1)
            pool.wait_ge(m_made, 1)
            nc.gpsimd.affine_select(out=m_ident[:, :], in_=m_ident[:, :], compare_op=ALU.not_equal, fill=1.0,
                                    base=0, pattern=[[-1, P]], channel_multiplier=1).then_inc(m_made, 1)

            def row_rstd(ready, done, n, t):
                pool.wait_ge(ready, n + 1)
                for i, (a, const, op) in enumerate(((m_ssq, m_inv_d, ALU.mult), (m_rstd, m_eps, ALU.add),
                                                    (m_rstd, m_neg_half, ALU.pow))):
                    if i > 0:
                        pool.wait_ge(done, 3 * n + i)
                    nc.gpsimd.tensor_tensor(m_rstd[:, t:t + 1], a[:, t:t + 1], const[:, :], op).then_inc(done, 1)

            for half in range(NH):
                for t in range(HT):
                    if half > 0:
                        pool.wait_ge(fin_ok, (half - 1) * HT + t + 1)
                    row_rstd(sq_ok, rs_ok, half * HT + t, t)
                with pool.Fori(half * NF, (half + 1) * NF) as f:
                    for i in range(2 * FT):
                        pool.wait_ge(m_hi_ok, f * 2 * FT + i + 1)
                        nc.gpsimd.tensor_tensor(m_lo[:, i, :], raw[:, i, :], m_hi[:, i, :].bitcast(F32),
                                                ALU.subtract).then_inc(m_lo_ok, 1)
                for t in range(HT):
                    pool.wait_ge(hn_ok, half * HT + t + 1)
                    row_rstd(fsq_ok, frs_ok, half * HT + t, t)

        @block.scalar
        def _(act):
            def split_hi(f, i):
                act.wait_ge(m_ld[i], (f + 1) * 16)
                nc.scalar.activation(m_hi[:, i, :], raw[:, i, :], ACT.Copy).then_inc(m_hi_ok, 1)

            def ff(half, f, i):
                act.wait_ge(up_pe, up_n(half, f) + i + 1)
                if i == 0:
                    act.wait_ge(add_ok, add_n(half, f))
                nc.scalar.activation(relu[:, i, :], ps[:, i, :], ACT.Relu).then_inc(relu_ok, 1)

            def ff_high(f, i):
                t, q = i // 2, i % 2
                act.wait_ge(sqr_ok, f * 4 + i + 1)
                nc.scalar.activation(ff_hi[:, t, q * 512:(q + 1) * 512], relu[:, i, :], ACT.Copy).then_inc(ff_hi_ok, 1)

            for half in range(NH):
                for t in range(HT):
                    n = half * HT + t
                    act.wait_ge(h_ld, (n + 1) * 16)
                    if n > 0:
                        act.wait_ge(sq_ok, n)
                    if half > 0:
                        act.wait_ge(fsq_ok, half * HT)
                        act.wait_ge(frs_ok, half * HT * 3)
                    nc.scalar.activation(m_junk[:, :], h_sb[:, t, :], ACT.Square,
                                         accum_out=m_ssq[:, t:t + 1]).then_inc(sq_ok, 1)
                    for g in range(2):
                        act.wait_ge(up_pe, half * NF * 4 + 2 * n + g + 1)
                        nc.scalar.activation(hT_hi[:, g * 4:g * 4 + 4, t * P:(t + 1) * P],
                                             ps[:, (2 * n + g) % 8, :].rearrange("p (k c) -> p k c", c=P),
                                             ACT.Copy).then_inc(relu_ok, 1)
                with act.Fori(half * NF, (half + 1) * NF) as f:
                    for i in range(FT):
                        act.wait_ge(up_pe, up_n(half, f))
                        split_hi(f, i)
                    act.wait_ge(add_ok, add_n(half, f))
                    for i in range(FT, 2 * FT):
                        split_hi(f, i)
                    for i in range(4):
                        ff(half, f, i)
                        ff_high(f, i)
                for t in range(HT):
                    n = half * HT + t
                    act.wait_ge(add_ok, add_n(half, (half + 1) * NF))
                    act.wait_ge(sq_ok, (half + 1) * HT)
                    act.wait_ge(rs_ok, (half + 1) * HT * 3)
                    if n > 0:
                        act.wait_ge(fsq_ok, n)
                    nc.scalar.activation(m_junk[:, :], h_sb[:, t, :], ACT.Square,
                                         accum_out=m_ssq[:, t:t + 1]).then_inc(fsq_ok, 1)

        @block.vector
        def _(dve):
            dve.wait_ge(rows_ld, 32)
            for half in range(NH):
                for t in range(HT):
                    n = half * HT + t
                    dve.wait_ge(rs_ok, 3 * (n + 1))
                    if n >= 2:
                        dve.wait_ge(up_pe, half * NF * 4 + 2 * (n - 1))
                    nc.vector.scalar_tensor_tensor(out=hn[:, t % 2, :], in0=h_sb[:, t, :], scalar=m_rstd[:, t:t + 1],
                                                   in1=g2_row[:, :], op0=ALU.mult, op1=ALU.mult).then_inc(hn_ok, 1)
                    for g in range(2):
                        dve.wait_ge(relu_ok, half * NF * 4 + 2 * n + g + 1)
                        at = (slice(None), slice(g * 4, g * 4 + 4), slice(t * P, (t + 1) * P))
                        nc.vector.tensor_tensor(hT_lo[at], ps[:, (2 * n + g) % 8, :].rearrange("p (k c) -> p k c", c=P),
                                                hT_hi[at].bitcast(F32), ALU.subtract).then_inc(add_ok, 1)
                with dve.Fori(half * NF, (half + 1) * NF) as f:
                    for i in range(4):
                        t, q = i // 2, i % 2
                        dve.wait_ge(relu_ok, up_n(half, f) + i + 1)
                        nc.vector.tensor_tensor(relu[:, i, :], relu[:, i, :], relu[:, i, :], ALU.mult).then_inc(sqr_ok, 1)
                        dve.wait_ge(ff_hi_ok, f * 4 + i + 1)
                        c = slice(q * 512, (q + 1) * 512)
                        nc.vector.tensor_tensor(ff_lo[:, t, c], relu[:, i, :], ff_hi[:, t, c].bitcast(F32),
                                                ALU.subtract).then_inc(ff_lo_ok, 1)
                    for n in range(NG):
                        t, c = n // 2, slice(n % 2 * 512, n % 2 * 512 + 512)
                        dve.wait_ge(down_pe, f * NG + n + 1)
                        nc.vector.tensor_tensor(h_sb[:, t, c], ps[:, 4 + n % 4, :], h_sb[:, t, c],
                                                ALU.add).then_inc(add_ok, 1)
                for t in range(HT):
                    n = half * HT + t
                    dve.wait_ge(frs_ok, 3 * (n + 1))
                    nc.vector.scalar_tensor_tensor(out=h_sb[:, t, :], in0=h_sb[:, t, :], scalar=m_rstd[:, t:t + 1],
                                                   in1=gf_row[:, :], op0=ALU.mult, op1=ALU.mult).then_inc(fin_ok, 1)

        @block.tensor
        def _(pe):
            pe.wait_ge(m_made, 2)
            for half in range(NH):
                for t in range(HT):
                    n = half * HT + t
                    pe.wait_ge(hn_ok, n + 1)
                    for g in range(2):
                        i = 2 * n + g
                        if half > 0 and t < 4:
                            pe.wait_ge(add_ok, add_n(half - 1, half * NF))
                        elif t >= 4:
                            pe.wait_ge(add_ok, half * NF * NG + i - 7)
                        for k in range(4):
                            kk = g * 4 + k
                            ins = nc.tensor.transpose(ps[:, i % 8, k * P:(k + 1) * P], hn[:, t % 2, kk * P:(kk + 1) * P],
                                                      m_ident[:, :])
                        ins.then_inc(up_pe, 1)
                pe.wait_ge(add_ok, add_n(half, half * NF))
                with pe.Fori(half * NF, (half + 1) * NF) as f:
                    for i in range(4):
                        t, q = i // 2, i % 2
                        if q == 0:
                            pe.wait_ge(m_lo_ok, f * 2 * FT + t + 1)
                        pe.wait_ge(relu_ok, up_n(half, f))
                        for k in range(KT):
                            c = slice(k * P, (k + 1) * P)
                            ins = three_products(nc, ps[:, i, :], m_hi[:, t, c], m_lo[:, t, c],
                                                 hT_hi[:, k, q * 512:(q + 1) * 512], hT_lo[:, k, q * 512:(q + 1) * 512],
                                                 k == 0, k == KT - 1)
                        ins.then_inc(up_pe, 1)
                    pe.wait_ge(m_lo_ok, (f + 1) * 2 * FT)
                    for n in range(NG):
                        t, q = n // 2, n % 2
                        c = slice(q * 512, (q + 1) * 512)
                        r = slice(t * P, (t + 1) * P)
                        if n == 0:
                            pe.wait_ge(ff_lo_ok, f * 4 + 3)
                        if n == NG // 2:
                            pe.wait_ge(ff_lo_ok, f * 4 + 4)
                        pe.wait_ge(add_ok, add_n(half, f) + max(n - 3, 0))
                        for i in range(FT):
                            o = ps[:, 4 + n % 4, :]
                            nc.tensor.matmul(o, ff_hi[:, i, r], m_hi[:, FT + i, c], start=(i == 0), stop=False)
                            nc.tensor.matmul(o, ff_hi[:, i, r], m_lo[:, FT + i, c], start=False, stop=False)
                            ins = nc.tensor.matmul(o, ff_lo[:, i, r], m_hi[:, FT + i, c], start=False, stop=(i == FT - 1))
                        ins.then_inc(down_pe, 1)


def hybrid_block(nc, x, norm1_g, w_in, w_gate_up, b_gate, gla_norm_g, conv_w, conv_b, conv_norm_g,
                 conv_norm_b, w_out, norm2_g, w_mlp_in, w_mlp_out, final_norm_g, out):
    h_dram = nc.dram_tensor("h_dram", [SEQ, D_MODEL], F32).ap()
    mixer_block(nc, x, norm1_g, w_in, w_gate_up, b_gate, gla_norm_g, conv_w, conv_b, conv_norm_g,
                conv_norm_b, w_out, h_dram)
    mlp_block(nc, h_dram, norm2_g, w_mlp_in, w_mlp_out, final_norm_g, out)


_INS = ["x", "norm1_g", "w_in", "w_gate_up", "b_gate", "gla_norm_g", "conv_w", "conv_b", "conv_norm_g",
        "conv_norm_b", "w_out", "norm2_g", "w_mlp_in", "w_mlp_out", "final_norm_g"]


_PER_CHANNEL = ["b_gate", "gla_norm_g", "conv_w", "conv_b", "conv_norm_g", "conv_norm_b"]


def kernel(**inputs):
    import numpy as np
    import concourse.bacc as bacc
    from concourse.bass_utils import run_bass_kernel_spmd

    nc = bacc.Bacc("TRN2", target_bir_lowering=False, num_devices=1)
    arrays, args = {}, []
    for name in _INS:
        a = np.ascontiguousarray(inputs[name])
        if name != "final_norm_g":
            a = a.reshape(a.shape[1:])
        if name in _PER_CHANNEL:
            a = a.reshape(a.shape[:-1] + (-1, P))
            a = np.ascontiguousarray(np.moveaxis(a, (-1, -2), (0, 1)))
        arrays[f"in_{name}"] = a
        args.append(nc.dram_tensor(f"in_{name}", a.shape, mybir.dt.from_np(a.dtype), kind="ExternalInput").ap())
    out = nc.dram_tensor("out_h", [SEQ, D_MODEL], F32, kind="ExternalOutput").ap()
    hybrid_block(nc, *args, out)
    r = run_bass_kernel_spmd(nc, [arrays], core_ids=[0])
    return r.results[0]["out_h"].reshape(1, SEQ, D_MODEL)
```

```python
from contextlib import ExitStack

import concourse.bass as bass
from concourse import mybir

F32 = mybir.dt.float32
F32R = mybir.dt.float32r
BF16 = mybir.dt.bfloat16
I32 = mybir.dt.int32
ALU = mybir.AluOpType
ACT = mybir.ActivationFunctionType

P = 128
D_MODEL = 1024
SEQ = 2048
HEADS = 4
DV = 128
DK = 64
KEY = HEADS * DK
VAL = HEADS * DV
RANK = 16
TAU = 16.0
CONV_CH = D_MODEL - VAL
CONV_GROUP = CONV_CH // 8
TAPS = 31
HALO = TAPS - 1
D_FF = 4 * D_MODEL
EPS = 1e-6
OFF_Q = 0
OFF_K = OFF_Q + KEY
OFF_V = OFF_K + KEY
OFF_G = OFF_V + VAL
OFF_A = OFF_G + VAL
OFF_C = OFF_A + RANK

KT = D_MODEL // P
BLK = 512
NB = SEQ // BLK
TT = BLK // P
CT = CONV_CH // P
PAIRS = HEADS // 2
LEVELS = [64, 32, 16, 8, 4, 2, 1]
NL = len(LEVELS)
NE = NL + 2

UNIT = 512
STAGES = 4
SLOTS = 4
CONV_UNITS = 2 * 2 * CT
FRONT_UNITS = CONV_UNITS + 2 * (KEY // P) * 2 + KT + 2 * HEADS
OUT_UNITS = 2 * KT
BLOCK_UNITS = FRONT_UNITS + OUT_UNITS
OUT_END = BLOCK_UNITS - CONV_UNITS

HALF = 1024
NH = SEQ // HALF
HT = HALF // P
FC = 256
FT = FC // P
HN = 2 * FT
NF = D_FF // FC


def three_products(nc, out, w_hi, w_lo, x_hi, x_lo, first, last):
    nc.tensor.matmul(out, w_hi, x_hi, start=first, stop=False)
    nc.tensor.matmul(out, w_hi, x_lo, start=False, stop=False)
    return nc.tensor.matmul(out, w_lo, x_hi, start=False, stop=last)


ALL_TAPS = TAPS * CT
EARLY_STEPS = 2
EARLY_TAPS = 16
FIRST_TAPS = 48
MORE_TAPS = 0.4
DECAY0_AT = [0, 1, 2]
GN_AT = [3]
V_GLA = 16
GLA_SPAN = 8.3
GLA_SPAN_START = 5.5
GLA_SPAN_END = 5.5
DECAYED_AT = 2.7
GN_UNITS = [0.5, 2, 3.6]
CN_UNITS = [2, 4, 5, 6, 7, 8, 9, 11, 13]


def block_steps(mix, nxt):
    before = (lambda *x: [x]) if mix else (lambda *x: [])
    unit = 0

    def take(name, arg, n):
        nonlocal unit
        unit += n
        return (name, arg, unit - n, n)

    s = [("x_load", 0), ("x_load", 1)] if nxt else []
    s += [("z",), take("qk", 0, 2), ("gate", 0), take("qk", 1, 2), ("gate", 1)] + before("gn_mixed", 0)
    s += [("decay",), ("gla_expo", 0), take("qk", 2, 2)] + before("gn_mixed", 1)
    s += [take("qk", 3, 2), ("gla_factors", 0)]
    fill = []
    for k in range(KT):
        fill += [take("v", k, 1)]
        if k in DECAY0_AT:
            fill += [("gla_decayed", 0, DECAY0_AT.index(k))]
        if k in GN_AT:
            fill += before("gn_mixed", 2 + GN_AT.index(k))
    fill += [("v_done", unit - 1)]
    for i in range(len(GN_AT), 2):
        fill += before("gn_mixed", 2 + i)
    v_end = unit

    gates = [take("g", h, 2) for h in range(HEADS)]
    if nxt:
        gates[1:1] = [("x_sq", 0)]
        gates[3:3] = [("x_norm", 0), ("x_sq", 1)]
        gates[6:6] = [("x_norm", 1)]
        gates += [("x_tr", 0), ("x_load", 2), ("x_tr", 1), ("x_load", 3)]
    fill += gates
    prep = [("x_sq", 2), ("x_norm", 2), ("x_sq", 3), ("x_norm", 3)] if nxt else []
    if mix:
        half0 = [take("out", (0, k), 1) for k in range(KT)]
        fill += half0[:1] + prep[:1] + half0[1:2] + prep[1:3] + half0[2:3] + [("res_load", 0)] + prep[3:] + half0[3:]
        fill += [("out_done", 0, unit - 1)]
        prep = []
    fill += prep
    if nxt:
        fill += [("x_tr", 2), ("x_tr", 3)]
    if mix:
        half1 = [take("out", (1, k), 1) for k in range(KT)]
        fill += half1[:2] + [("store", 0)] + half1[2:4] + [("res_load", 1)] + half1[4:]
        fill += [("out_done", 1, unit - 1), ("store", 1)]
    taps_end = unit
    if nxt:
        for j in range(CT):
            fill += [take("conv_gate", j, 2), take("conv_in", j, 2)]
    end = unit

    start, span = (V_GLA, GLA_SPAN) if mix and nxt else (V_GLA, GLA_SPAN_START if nxt else GLA_SPAN_END)
    events = []
    for c in range(TT):
        o, r = start + span * c, span / 9
        if c + 1 < TT:
            events += [(o, ("gla_expo", c + 1))]
        events += [(o, ("gla_scores", c, 0)), (o, ("gla_select", c, 0))]
        if c + 1 < TT:
            events += [(o + 1 * r, ("gla_factors", c + 1))]
        events += [(o + 2 * r, ("gla_scores", c, 1)), (o + 2 * r, ("gla_select", c, 1))]
        if c + 1 < TT:
            events += [(o + (DECAYED_AT + i) * r, ("gla_decayed", c + 1, i)) for i in range(3)]
        events += [(max(o + 4.5 * r, v_end + 0.5), ("gla_out", c))]
    last = events[-1][0]
    events += [(last + u, (n,)) for u, n in zip(GN_UNITS, ("gn_square", "gn_sum", "gn_rstd"))]
    cn = [("cn_mean", 0), ("cn_mean", 1), ("cn_var", 0), ("cn_var", 1)]
    cn += [("cn_rstd",)] + [("cn_mixed", j) for j in range(CT)]
    cn_units = CN_UNITS if nxt else [0.2] * len(cn)
    events += [(taps_end + u, e) for u, e in zip(cn_units, cn)]
    events.sort(key=lambda e: e[0])

    at = fill[0][2]
    filled = []
    for f in fill:
        while events and len(f) == 4 and events[0][0] <= at:
            filled.append(events.pop(0)[1])
        filled.append(f)
        if len(f) == 4:
            at += f[3]
    s += filled + [e for _, e in events]

    def share(u):
        return u + MORE_TAPS * min(u, v_end)

    done = EARLY_TAPS if mix else FIRST_TAPS
    todo, steps = done, []
    early_from = end - 2 * EARLY_STEPS
    for f in s:
        steps.append(f)
        if len(f) == 4 or f[0] == "out_done":
            last = f[2] + (f[3] if len(f) == 4 else 1)
            if f[0] == "out" and f[1][1] == KT - 1:
                continue
            if last <= taps_end:
                n = done + int((ALL_TAPS - done) * share(last) / share(taps_end)) - todo
                if n > 0:
                    steps.append(("taps", todo, n))
                    todo += n
            elif last > early_from:
                n = EARLY_TAPS // EARLY_STEPS
                steps.append(("early_taps", (last - early_from) // 2 * n - n, n))
    assert todo == ALL_TAPS
    return steps


def first_steps():
    s = []
    for j in range(CT):
        s += [("conv_gate", j, 4 * j, 2), ("conv_in", j, 4 * j + 2, 2)] + ([("make_wz",)] if j == 1 else [])
        if j >= CT // 2:
            s[-1:] = [("early_taps", (j - CT // 2) * FIRST_TAPS // 2, FIRST_TAPS // 4), s[-1],
                      ("early_taps", (2 * j - CT + 1) * FIRST_TAPS // 4, FIRST_TAPS // 4)]
    return s


def last_steps(end):
    i = end.index(("cn_mean", 0))
    cn = [(e, NB - 1) for e in end[i:]]
    assert all(e[0].startswith("cn_") for e in end[i:])
    unit = 0
    out = {}
    for half, ks in ((0, range(HEADS)), (1, range(HEADS)), (0, range(HEADS, KT)), (1, range(HEADS, KT))):
        for k in ks:
            out[half, k] = (("out", (half, k), unit, 1), NB)
            unit += 1
    gn = [(("gn_mixed", h), NB) for h in range(HEADS)]
    s = [gn[0], gn[1], cn[0], gn[2], cn[1], gn[3], (("res_load", 0), NB)]
    s += [out[0, 0], cn[2], out[0, 1], cn[3], out[0, 2], out[0, 3]]
    s += cn[HEADS:] + [(("res_load", 1), NB)] + [out[1, k] for k in range(HEADS)]
    for half in range(2):
        s += [out[half, k] for k in range(HEADS, KT)]
        s += [(("out_done", half, out[half, KT - 1][0][2]), NB), (("store", half), NB)]
    return end[:i], s


def mixer_block(nc, x, norm1_g, w_in, w_gate_up, b_gate, gla_norm_g, conv_w, conv_b,
                conv_norm_g, conv_norm_b, w_out, h_dram, h_st):
    with ExitStack() as ctx:
        def sb(name, shape, dt=F32):
            return ctx.enter_context(nc.sbuf_tensor(name, shape, dt))

        def sem(name):
            return ctx.enter_context(nc.semaphore(name))

        x_nat = sb("x_nat", [P, 2, D_MODEL])
        g1_row = sb("g1_row", [P, D_MODEL])
        ssq = sb("ssq", [P, TT])
        rstd = sb("rstd", [P, TT])
        neg_half = sb("neg_half", [P, 1])
        eps_col = sb("eps_col", [P, 1])
        inv_d = sb("inv_d", [P, 1])
        pace = sb("pace", [P, 1])
        one_col = sb("one_col", [P, 1])
        head_cols = sb("head_cols", [P, 2])
        xT_hi = sb("xT_hi", [P, KT, BLK], F32R)
        xT_lo = sb("xT_lo", [P, KT, BLK], F32R)
        w_raw = sb("w_raw", [P, STAGES, UNIT])
        w_hi = sb("w_hi", [P, SLOTS, UNIT], F32R)
        w_lo = sb("w_lo", [P, SLOTS, UNIT], F32R)
        wz_raw = sb("wz_raw", [P, KT, RANK])
        wz = sb("wz", [P, KT, 2, RANK], F32R)
        w_up = sb("w_up", [2 * RANK, KEY])
        bg_col = sb("bg_col", [P, PAIRS])
        q_sb = sb("q_sb", [P, PAIRS, BLK])
        k_sb = sb("k_sb", [P, PAIRS, BLK])
        cum = sb("cum", [P, PAIRS, BLK])
        v_sb = sb("v_sb", [P, TT, VAL])
        silu_g = sb("silu_g", [P, HEADS, BLK])
        sig = sb("sig", [P, 2, BLK])
        log1p_t = sig
        z_sb = sig[0:2 * RANK, 1, :]
        u_sb = sb("u_sb", [P, CT, HALO + BLK])
        y_sb = sb("y_sb", [P, CT, BLK])
        o_sb = sb("o_sb", [P, HEADS, BLK])
        res_sb = sb("res_sb", [P, TT, 512])
        nr = res_sb
        junk = res_sb[:, 0:2, :].rearrange("p a c -> p (a c)")
        mix_hi = sb("mix_hi", [P, KT, BLK], F32R)
        mix_lo = sb("mix_lo", [P, KT, BLK], F32R)
        fac = sb("fac", [P, NE, PAIRS, P])
        gn_r = fac[:, 0:NE - 1, :, :].rearrange("p e a c -> p (e a c)").rearrange("p (h t) -> p h t", h=HEADS)
        ke = sb("ke", [P, NL, PAIRS, P])
        qe = sb("qe", [P, NL, PAIRS, P // 2])
        qe_head = sb("qe_head", [P, NL, PAIRS, 2, P // 2])
        k_end = sb("k_end", [P, PAIRS, P])
        q_in = sb("q_in", [P, 2, PAIRS, P])
        decay = sb("decay", [P, 2, PAIRS])
        qk = sb("qk", [P, PAIRS, P])
        k_endT = sb("k_endT", [P, PAIRS, P])
        probs = sb("probs", [P, HEADS, P])
        state = sb("state", [P, HEADS, DV])
        lvl_mask = sb("lvl_mask", [P, NL, P // 2])
        ident = sb("ident", [P, P])
        mean_dv = sb("mean_dv", [P, P])
        mean_grp = sb("mean_grp", [P, P])
        cw_col = sb("cw_col", [P, CT, TAPS])
        cb_col = sb("cb_col", [P, CT])
        cg_col = sb("cg_col", [P, CT])
        cnb_col = sb("cnb_col", [P, CT])
        gn_col = sb("gn_col", [P, 1])
        acc = ctx.enter_context(nc.psum_tensor("acc", [P, 8, 512], F32))

        g1_ld = sem("g1_ld")
        consts_ld = sem("consts_ld")
        made = sem("made")
        w_ld = [sem(f"w_ld{i}") for i in range(STAGES)]
        w_hi_ok = sem("w_hi_ok")
        w_lo_ok = sem("w_lo_ok")
        w_used = sem("w_used")
        wz_ok = sem("wz_ok")
        x_ld = [sem(f"x_ld{i}") for i in range(TT)]
        x_ssq = sem("x_ssq")
        x_rstd = sem("x_rstd")
        x_norm = sem("x_norm")
        xt_pe = sem("xt_pe")
        xt_hi_ok = sem("xt_hi_ok")
        low_ok = sem("low_ok")
        sum_ok = sem("sum_ok")
        z_pe = sem("z_pe")
        gate_pe = sem("gate_pe")
        csig_ok = sem("csig_ok")
        u_ok = sem("u_ok")
        z_ok = sem("z_ok")
        gate_act = sem("gate_act")
        gate_min = sem("gate_min")
        cum_ok = sem("cum_ok")
        qk_ok = sem("qk_ok")
        v_pe = sem("v_pe")
        v_ok = sem("v_ok")
        gsig_ok = sem("gsig_ok")
        silu_ok = sem("silu_ok")
        tap_ok = sem("tap_ok")
        cn_mean_pe, cn_dev, cn_sq, cn_var_pe, cn_rs, cn_n, cn_sig, cn_aff, cn_f, cn_hi, cn_lo = (
            sem(n) for n in ("cn_mean_pe", "cn_dev", "cn_sq", "cn_var_pe", "cn_rs", "cn_n",
                             "cn_sig", "cn_aff", "cn_f", "cn_hi", "cn_lo"))
        gn_sq, gn_sum_pe, gn_rs, gn_n, gn_f, gn_hi, gn_lo = (
            sem(n) for n in ("gn_sq", "gn_sum_pe", "gn_rs", "gn_n", "gn_f", "gn_hi", "gn_lo"))
        expo_ok = sem("expo_ok")
        fac_ok = sem("fac_ok")
        ke_ok = sem("ke_ok")
        qe_ok = sem("qe_ok")
        score_pe = sem("score_pe")
        kT_pe = sem("kT_pe")
        kT_ok = sem("kT_ok")
        probs_ok = sem("probs_ok")
        o_pe = sem("o_pe")
        o_ok = sem("o_ok")
        upd_pe = sem("upd_pe")
        state_ok = sem("state_ok")
        out_pe = sem("out_pe")
        res_ld = [sem(f"res_ld{i}") for i in range(2)]
        block = ctx.enter_context(nc.Block())

        FIRST = first_steps()
        START = block_steps(False, True)
        BODY = block_steps(True, True)
        END, LAST = last_steps(block_steps(True, False))

        def base(b):
            if isinstance(b, int) and b <= 0:
                return 0 if b < 0 else CONV_UNITS
            return b * BLOCK_UNITS if not (isinstance(b, int) and b == NB) else NB * BLOCK_UNITS - OUT_UNITS

        def run(eng, do):
            for s in FIRST:
                do(s, -1)
            for s in START:
                do(s, 0)
            with eng.Fori(1, NB - 1) as b:
                for s in BODY:
                    do(s, b)
            for s in END:
                do(s, NB - 1)
            for s, b in LAST:
                do(s, b)

        LAST_UNIT = NB * BLOCK_UNITS
        assert all(n % STAGES == 0 for n in (CONV_UNITS, FRONT_UNITS, OUT_UNITS))
        LOWS = 2 * TT

        def first(b):
            return isinstance(b, int) and b <= 0

        def out_bank(b, half, t):
            return (LAST_OUT_BANK if last(b) else OUT_BANK)[half][t]

        def last(b):
            return isinstance(b, int) and b == NB

        def res(m, half):
            return o_sb if isinstance(m, int) and m == NB - 1 and half == 0 else res_sb

        def x_tile(m, t):
            if isinstance(m, int) and m == 0 and t >= 2:
                return o_sb[:, 2 * t - 4:2 * t - 2, :].rearrange("p a c -> p (a c)")
            return x_nat[:, t % 2, :]

        def trailing(i, n):
            return ([i - 1] if i > 0 else []) + ([i] if i == n - 1 else [])

        def pair(step):
            return range(step[1] * 2, step[1] * 2 + 2)

        w_in_t = w_in.rearrange("(k p) e -> p k e", p=P)
        w_out_t = w_out.rearrange("(k p) e -> p k e", p=P)
        x_t = x.rearrange("(n p) d -> p n d", p=P)
        h_t = h_dram.rearrange("(n p) d -> p n d", p=P)

        def sources(steps):
            out = []
            for step in steps:
                name = step[0]
                if name in ("conv_gate", "conv_in", "qk", "g"):
                    off = {"conv_gate": OFF_C + CONV_CH, "conv_in": OFF_C, "qk": OFF_Q, "g": OFF_G}[name] + step[1] * P
                    out += [w_in_t[:, i * 4:i * 4 + 4, off:off + P] for i in range(2)]
                elif name == "v":
                    out += [w_in_t[:, step[1], OFF_V:OFF_V + VAL]]
                elif name == "out":
                    half, k = step[1]
                    out += [w_out_t[:, k, half * 512:half * 512 + 512]]
            return out

        STREAMS = [sources(steps) for steps in (FIRST, START, BODY, END, [s for s, _ in LAST])]
        assert [len(u) for u in STREAMS] == [CONV_UNITS, FRONT_UNITS, BLOCK_UNITS, OUT_END, OUT_UNITS]

        @block.sync
        def _(sp):
            def load(n, src, before):
                if before is not None:
                    sp.wait_ge(w_lo_ok, before)
                dst = w_raw[:, n % STAGES, :]
                if len(src.shape) == 3:
                    dst = dst.rearrange("p (k e) -> p k e", e=P)
                sp.dma_start(dst, src).then_inc(w_ld[n % STAGES], 16)

            def load_ahead(b, i):
                n = i + SLOTS + STAGES
                kind = 2 if not isinstance(b, int) else b + 1 if b < 1 else b
                if n < len(STREAMS[kind]):
                    src = STREAMS[kind][n]
                elif kind < 4:
                    src = STREAMS[kind + 1][n - len(STREAMS[kind])]
                else:
                    return
                load(n, src, base(b) + n - STAGES + 1)

            def x_load(b, t):
                if not (isinstance(b, int) and b == 0):
                    sp.wait_ge(xt_pe, b * 2 * TT + 2 * (t - 1))
                if isinstance(b, int):
                    src = x_t[:, b * TT + t, :]
                else:
                    src = x_t[:, bass.ds(b * TT + t, 1), :].rearrange("p a d -> p (a d)")
                sp.dma_start(x_tile(b, t), src).then_inc(x_ld[t], 16)

            def tok(ap, b, half):
                if isinstance(b, int):
                    return ap[:, b * TT:b * TT + TT, half * 512:half * 512 + 512]
                return ap[:, bass.ds(b * TT, TT), half * 512:half * 512 + 512]

            def res_load(m, half):
                if last(m + 1):
                    sp.wait_ge(*((gn_lo, NB * HEADS) if half == 0 else (cn_f, NB * CT)))
                elif half == 0:
                    sp.wait_ge(cn_f, (m + 1) * CT)
                    sp.wait_ge(x_ssq, NB * TT if isinstance(m, int) else (m + 3) * TT)
                else:
                    sp.wait_ge(h_st, (m * 2 + half + 1) * 16)
                sp.dma_start(res(m, half)[:, :, :], tok(x_t, m, half)).then_inc(res_ld[half], 16)

            def h_store(m, half):
                sp.wait_ge(sum_ok, m * LOWS + (half + 1) * TT)
                sp.dma_start(tok(h_t, m, half), res(m, half)[:, :, :]).then_inc(h_st, 16)

            def do(step, b):
                name = step[0]
                if name in ("conv_gate", "conv_in", "qk", "g", "v", "out"):
                    for i in range(step[3]):
                        load_ahead(b, step[2] + i)
                elif name == "x_load":
                    x_load(b + 1, step[1])
                elif name == "res_load":
                    res_load(b - 1, step[1])
                elif name == "store":
                    h_store(b - 1, step[1])

            x_load(0, 0)
            sp.dma_start(g1_row[:, :], norm1_g.partition_broadcast(P)).then_inc(g1_ld, 16)
            for t in range(1, TT):
                x_load(0, t)
                load(t - 1, STREAMS[0][t - 1], None)
            for n in range(TT - 1, STAGES):
                load(n, STREAMS[0][n], None)
            sp.dma_start(wz_raw[:, :, :], w_in_t[:, :, OFF_A:OFF_A + RANK]).then_inc(consts_ld, 16)
            for r in range(2):
                sp.dma_start(w_up[r * RANK:(r + 1) * RANK, :], w_gate_up).then_inc(consts_ld, 16)
            for dst, src in ((bg_col, b_gate), (cb_col, conv_b), (cg_col, conv_norm_g), (cnb_col, conv_norm_b)):
                sp.dma_start(dst[:, :], src).then_inc(consts_ld, 16)
            sp.dma_start(gn_col[:, :], gla_norm_g).then_inc(h_st, 16)
            sp.dma_start(cw_col[:, :, :], conv_w).then_inc(consts_ld, 16)
            for n in range(STAGES, STAGES + SLOTS):
                load(n, STREAMS[0][n], n - STAGES + 1)
            run(sp, do)

        @block.gpsimd
        def _(pool):
            n_made = [0]

            def mk(ins):
                n_made[0] += 1
                ins.then_inc(made, 1)

            mk(nc.gpsimd.memset(ident[:, :], 0.0))
            mk(nc.gpsimd.memset(neg_half[:, :], -0.5))
            mk(nc.gpsimd.memset(eps_col[:, :], EPS))
            mk(nc.gpsimd.memset(inv_d[:, :], 1.0 / D_MODEL))
            pool.wait_ge(made, n_made[0])
            mk(nc.gpsimd.affine_select(out=ident[:, :], in_=ident[:, :], compare_op=ALU.not_equal, fill=1.0,
                                       base=0, pattern=[[-1, P]], channel_multiplier=1))
            assert n_made[0] == MADE_IDENT

            def make_plain():
                mk(nc.gpsimd.memset(one_col[:, :], 1.0))
                mk(nc.gpsimd.memset(mean_dv[:, :], 1.0 / DV))
                mk(nc.gpsimd.memset(mean_grp[:, :], 0.0))
                mk(nc.gpsimd.memset(lvl_mask[:, :, :], 1.0))
                mk(nc.gpsimd.memset(head_cols[:, :], 0.0))
                mk(nc.gpsimd.memset(u_sb[:, :, BLK:BLK + HALO], 0.0))
                mk(nc.gpsimd.memset(state[:, :, :], 0.0))
                mk(nc.gpsimd.memset(probs[:, :, :], 0.0))

            def make_zero_parts():
                mk(nc.gpsimd.memset(ke[:, :, :, :], 0.0))
                mk(nc.gpsimd.memset(qe_head[:, :, :, :, :], 0.0))

            def make_patterns():
                pool.wait_ge(made, n_made[0])
                pool.wait_ge(x_rstd, 3 * TT)
                pool.wait_ge(w_lo_ok, SLOTS)
                for i in range(2):
                    mk(nc.gpsimd.memset(head_cols[i * DK:(i + 1) * DK, i:i + 1], 1.0))
                for g in range(P // CONV_GROUP):
                    r = slice(g * CONV_GROUP, (g + 1) * CONV_GROUP)
                    mk(nc.gpsimd.memset(mean_grp[r, r], 1.0 / CONV_GROUP))
                    pool.wait_ge(made, n_made[0])
                for lv, s in enumerate(LEVELS):
                    m = lvl_mask[:, lv, :].rearrange("p (n s) -> p n s", s=s)
                    n = P // (2 * s)
                    mk(nc.gpsimd.affine_select(out=m, in_=m, compare_op=ALU.is_ge, fill=0.0, base=0,
                                               pattern=[[-2 * s, n], [0, s]], channel_multiplier=1))
                pool.wait_ge(made, n_made[0])
                for lv, s in enumerate(LEVELS):
                    m = lvl_mask[:, lv, :].rearrange("p (n s) -> p n s", s=s)
                    n = P // (2 * s)
                    mk(nc.gpsimd.affine_select(out=m, in_=m, compare_op=ALU.is_ge, fill=0.0, base=s - 1,
                                               pattern=[[2 * s, n], [0, s]], channel_multiplier=-1))

            def split_lo(g, slot, stage):
                pool.wait_ge(w_hi_ok, g + 1)
                nc.gpsimd.tensor_tensor(w_lo[:, slot, :], w_raw[:, stage, :], w_hi[:, slot, :].bitcast(F32),
                                        ALU.subtract).then_inc(w_lo_ok, 1)

            def split_next(b, i):
                n = i + SLOTS
                if isinstance(b, int) and base(b) + n >= LAST_UNIT:
                    return
                split_lo(base(b) + n, n % SLOTS, n % STAGES)

            def x_rs(b, t):
                pool.wait_ge(x_ssq, b * TT + t + 1)
                for i, (a, const, op) in enumerate(((ssq, inv_d, ALU.mult), (rstd, eps_col, ALU.add),
                                                    (rstd, neg_half, ALU.pow))):
                    if i > 0:
                        pool.wait_ge(x_rstd, (b * TT + t) * 3 + i)
                    nc.gpsimd.tensor_tensor(rstd[:, t:t + 1], a[:, t:t + 1], const[:, :], op).then_inc(x_rstd, 1)

            def decayed_begin(b, c, t):
                pool.wait_ge(fac_ok, b * TT + c + 1)
                if c == 0:
                    pool.wait_ge(qk_ok, b * 4 + 4)
                if c > 0 or not first(b):
                    pool.wait_ge(score_pe, (b * TT + c) * PAIRS)
                    pool.wait_ge(kT_pe, b * TT + c)
                    pool.wait_ge(qe_ok, (b * TT + c) * 2)
                if c > 1:
                    pool.wait_ge(o_pe, b * TT + c - 1)
                elif not first(b):
                    pool.wait_ge(o_pe, b * TT + c - 1)
                nc.gpsimd.tensor_tensor(k_end[:, :, :], k_sb[:, :, t], fac[:, NL, :, :], ALU.mult)
                nc.gpsimd.tensor_tensor(q_in[:, c % 2, :, :], q_sb[:, :, t], fac[:, NL + 1, :, :], ALU.mult)
                nc.gpsimd.tensor_tensor(qk[:, :, :], q_sb[:, :, t], k_sb[:, :, t], ALU.mult)

            def do(step, b):
                name = step[0]
                if name in ("conv_gate", "conv_in", "qk", "g", "v", "out"):
                    for i in range(step[3]):
                        split_next(b, step[2] + i)
                elif name == "x_sq":
                    x_rs(b + 1, step[1])
                elif name == "gla_decayed":
                    c, part = step[1:]
                    t = slice(c * P, (c + 1) * P)
                    if part == 0:
                        decayed_begin(b, c, t)
                    for lv in (range(0, 1), range(1, 4), range(4, NL))[part]:
                        s = LEVELS[lv]
                        f4 = fac[:, lv, :, :].rearrange("p a (n h s) -> p a n h s", h=2, s=s)
                        k4 = k_sb[:, :, t].rearrange("p a (n h s) -> p a n h s", h=2, s=s)
                        q4 = q_sb[:, :, t].rearrange("p a (n h s) -> p a n h s", h=2, s=s)
                        o4 = ke[:, lv, :, :].rearrange("p a (n h s) -> p a n h s", h=2, s=s)
                        nc.gpsimd.tensor_tensor(o4[:, :, :, 0, :], k4[:, :, :, 0, :], f4[:, :, :, 0, :], ALU.mult)
                        ins = nc.gpsimd.tensor_tensor(qe[:, lv, :, :].rearrange("p a (n s) -> p a n s", s=s),
                                                      q4[:, :, :, 1, :], f4[:, :, :, 1, :], ALU.mult)
                    if part == 2:
                        ins.then_inc(ke_ok, 1)
                elif isinstance(b, int) and b == NB - 1 and name in ("cn_rstd", "cn_mixed"):
                    pass
                elif name == "cn_rstd":
                    for j in range(CT):
                        pool.wait_ge(cn_rs, b * CT * 2 + CT + j + 1)
                        nc.gpsimd.tensor_tensor(y_sb[:, j, :], y_sb[:, j, :], nr[:, j, :], ALU.mult).then_inc(cn_n, 1)
                elif name == "cn_mixed":
                    j = step[1]
                    pool.wait_ge(cn_sig, b * CT + j + 1)
                    pool.wait_ge(cn_aff, b * CT + j + 1)
                    nc.gpsimd.tensor_tensor(y_sb[:, j, :], y_sb[:, j, :], nr[:, j, :], ALU.mult).then_inc(cn_f, 1)
                    for i in trailing(j, CT):
                        pool.wait_ge(cn_hi, b * CT + i + 1)
                        nc.gpsimd.tensor_tensor(mix_lo[:, HEADS + i, :], y_sb[:, i, :],
                                                mix_hi[:, HEADS + i, :].bitcast(F32), ALU.subtract).then_inc(cn_lo, 1)
                elif name == "gn_mixed":
                    m, h = b - 1, step[1]
                    pool.wait_ge(gn_n, m * HEADS + h + 1)
                    nc.gpsimd.tensor_tensor(o_sb[:, h, :], o_sb[:, h, :], silu_g[:, h, :], ALU.mult).then_inc(gn_f, 1)
                    for i in trailing(h, HEADS):
                        pool.wait_ge(gn_hi, m * HEADS + i + 1)
                        nc.gpsimd.tensor_tensor(mix_lo[:, i, :], o_sb[:, i, :],
                                                mix_hi[:, i, :].bitcast(F32), ALU.subtract).then_inc(gn_lo, 1)

            for t in range(TT):
                x_rs(0, t)
                if t == 0:
                    make_plain()
            for g in range(SLOTS):
                split_lo(g, g, g)
            make_zero_parts()
            make_patterns()
            assert n_made[0] == MADE
            run(pool, do)

        @block.scalar
        def _(act):
            def split_hi(g, slot, stage, b, n):
                act.wait_ge(w_ld[stage], (stage_round(b, n) + 1) * 16)
                if not (isinstance(g, int) and g < SLOTS):
                    act.wait_ge(w_used, g - SLOTS + 1)
                nc.scalar.activation(w_hi[:, slot, :], w_raw[:, stage, :], ACT.Copy).then_inc(w_hi_ok, 1)

            def stage_round(b, n):
                if isinstance(b, int):
                    return (base(b) + n) // STAGES
                return b * (BLOCK_UNITS // STAGES) + n // STAGES

            def split_next(b, i):
                n = i + SLOTS
                if isinstance(b, int) and base(b) + n >= LAST_UNIT:
                    return
                split_hi(base(b) + n, n % SLOTS, n % STAGES, b, n)

            def x_sq(b, t):
                act.wait_ge(x_ld[t], (b + 1) * 16)
                if not (first(b) and t == 0):
                    act.wait_ge(x_ssq, b * TT + t)
                if not first(b):
                    act.wait_ge(x_norm, (b - 1) * TT + t + 1)
                    if not (isinstance(b, int) and b == 1):
                        act.wait_ge(cn_f, (b - 1) * CT)
                nc.scalar.activation(junk, x_tile(b, t), ACT.Square,
                                     accum_out=ssq[:, t:t + 1]).then_inc(x_ssq, 1)

            def xt_hi(b, t):
                for g in range(2):
                    act.wait_ge(xt_pe, b * 2 * TT + 2 * t + g + 1)
                    src = acc[:, X_BANKS[t][g], :].rearrange("p (k c) -> p k c", c=P)
                    nc.scalar.activation(xT_hi[:, g * 4:g * 4 + 4, t * P:(t + 1) * P], src,
                                         ACT.Copy).then_inc(xt_hi_ok, 1)

            def do(step, b):
                name = step[0]
                if name in ("conv_gate", "conv_in", "qk", "g", "v", "out"):
                    for i in range(step[3]):
                        split_next(b, step[2] + i)
                if name == "conv_gate":
                    m, j = b + 1, step[1]
                    act.wait_ge(w_used, base(b) + step[2] + 2)
                    if j >= 2:
                        act.wait_ge(u_ok, m * 2 * CT + 2 * (j - 1))
                    elif not first(m):
                        act.wait_ge(silu_ok, m * HEADS - 1 + j)
                    nc.scalar.activation(sig[:, j % 2, :], acc[:, 0, :], ACT.Sigmoid).then_inc(csig_ok, 1)
                elif name == "make_wz":
                    act.wait_ge(made, MADE)
                    act.wait_ge(consts_ld, CONSTS)
                    nc.scalar.activation(wz[:, :, 0, :], wz_raw[:, :, :], ACT.Copy).then_inc(wz_ok, 1)
                elif name == "z":
                    act.wait_ge(z_pe, b + 1)
                    act.wait_ge(u_ok, (b + 1) * 2 * CT)
                    if not first(b):
                        act.wait_ge(gate_pe, b * PAIRS)
                    nc.scalar.activation(z_sb, acc[0:2 * RANK, 0, :], ACT.Copy).then_inc(z_ok, 1)
                elif name == "gate":
                    j = step[1]
                    act.wait_ge(gate_pe, b * PAIRS + j + 1)
                    nc.scalar.activation(log1p_t[:, j, :], acc[:, 0, :], ACT.Abs,
                                         bias=bg_col[:, j:j + 1]).then_inc(gate_act, 1)
                elif name == "decay":
                    act.wait_ge(gate_act, b * 4 + 2)
                    nc.scalar.activation(log1p_t[:, :, :], log1p_t[:, :, :], ACT.Exp, scale=-1.0).then_inc(gate_act, 1)
                    act.wait_ge(gate_act, b * 4 + 3)
                    nc.scalar.activation(log1p_t[:, :, :], log1p_t[:, :, :], ACT.Ln,
                                         bias=one_col[:, :]).then_inc(gate_act, 1)
                elif name == "qk":
                    j = step[1]
                    act.wait_ge(w_used, base(b) + step[2] + 2)
                    if j == 0 and not first(b):
                        act.wait_ge(ke_ok, b * TT)
                    dst = (q_sb if j < PAIRS else k_sb)[:, j % PAIRS, :]
                    nc.scalar.activation(dst, acc[:, QK_BANK[j], :], ACT.Copy,
                                         scale=DK ** -0.5 if j < PAIRS else 1.0).then_inc(qk_ok, 1)
                elif name == "v_done":
                    if not first(b):
                        act.wait_ge(upd_pe, b * TT)
                    for t in range(TT):
                        if t < TT - 1:
                            act.wait_ge(v_pe, b * (TT - 1) + t + 1)
                        else:
                            act.wait_ge(w_used, base(b) + step[1] + 1)
                        nc.scalar.activation(v_sb[:, t, :], acc[:, V_BANK[t], :], ACT.Copy).then_inc(v_ok, 1)
                elif name == "g":
                    j = step[1]
                    act.wait_ge(w_used, base(b) + step[2] + 2)
                    if j >= 2:
                        act.wait_ge(silu_ok, b * HEADS + j - 1)
                    else:
                        act.wait_ge(cum_ok, (b + 1) * PAIRS * TT)
                    nc.scalar.activation(sig[:, j % 2, :], acc[:, G_BANK[j], :], ACT.Sigmoid).then_inc(gsig_ok, 1)
                elif name == "x_sq":
                    x_sq(b + 1, step[1])
                elif name == "x_tr":
                    xt_hi(b + 1, step[1])
                elif name == "gla_factors":
                    c = step[1]
                    act.wait_ge(expo_ok, b * TT + c + 1)
                    if c > 1 or not first(b):
                        act.wait_ge(state_ok, (b * TT + c - 1) * HEADS)
                    nc.scalar.activation(decay[:, c % 2, :], cum[:, :, (c + 1) * P - 1], ACT.Exp, scale=1.0 / TAU)
                    nc.scalar.activation(fac[:, 0:NL + 1, :, :], fac[:, 0:NL + 1, :, :], ACT.Exp, scale=1.0 / TAU)
                    nc.scalar.activation(fac[:, NL + 1, :, :], cum[:, :, c * P:(c + 1) * P], ACT.Exp,
                                         scale=1.0 / TAU).then_inc(fac_ok, 1)
                elif name == "gla_decayed" and step[2] == 2:
                    act.wait_ge(ke_ok, b * TT + step[1] + 1)
                    if step[1] > 0 or not first(b):
                        act.wait_ge(score_pe, (b * TT + step[1]) * PAIRS)
                    for i in range(2):
                        r = slice(i * DK, (i + 1) * DK)
                        nc.scalar.activation(qe_head[r, :, :, i, :], qe[r, :, :, :], ACT.Copy).then_inc(qe_ok, 1)
                elif name == "gla_scores" and step[2] == 0:
                    c = step[1]
                    act.wait_ge(kT_pe, b * TT + c + 1)
                    if c > 0 or not first(b):
                        act.wait_ge(upd_pe, b * TT + c)
                    nc.scalar.activation(k_endT[:, :, :], acc[:, 7, 0:KEY].rearrange("p (a c) -> p a c", c=P),
                                         ACT.Copy).then_inc(kT_ok, 1)
                elif name == "gla_out":
                    c = step[1]
                    act.wait_ge(o_pe, b * TT + c + 1)
                    if c == 0 and not first(b):
                        act.wait_ge(gn_lo, b * HEADS)
                    nc.scalar.activation(o_sb[:, :, c * P:(c + 1) * P], acc[:, 6, :].rearrange("p (h c) -> p h c", c=P),
                                         ACT.Copy).then_inc(o_ok, 1)
                elif name == "cn_mean":
                    if step[1] == 0 and not first(b):
                        act.wait_ge(h_st, (b * 2 + 1) * 16)
                    for j in pair(step):
                        act.wait_ge(cn_dev, b * CT + j + 1)
                        nc.scalar.activation(nr[:, j, :], y_sb[:, j, :], ACT.Square).then_inc(cn_sq, 1)
                elif name == "cn_var":
                    for j in pair(step):
                        act.wait_ge(cn_var_pe, b * CT + j + 1)
                        nc.scalar.activation(nr[:, j, :], acc[:, CN_BANK[j], :], ACT.Ln,
                                             bias=eps_col[:, :]).then_inc(cn_rs, 1)
                elif name == "cn_rstd":
                    for j in range(CT):
                        act.wait_ge(cn_rs, b * CT * 2 + j + 1)
                        nc.scalar.activation(nr[:, j, :], nr[:, j, :], ACT.Exp, scale=-0.5).then_inc(cn_rs, 1)
                elif name == "cn_mixed":
                    j = step[1]
                    act.wait_ge(cn_n, b * CT + j + 1)
                    nc.scalar.activation(nr[:, j, :], y_sb[:, j, :], ACT.Sigmoid, bias=cnb_col[:, j:j + 1],
                                         scale=cg_col[:, j:j + 1]).then_inc(cn_sig, 1)
                    if not first(b):
                        act.wait_ge(w_used, base(b) + OUT_END)
                    for i in trailing(j, CT):
                        act.wait_ge(cn_f, b * CT + i + 1)
                        nc.scalar.activation(mix_hi[:, HEADS + i, :], y_sb[:, i, :], ACT.Copy).then_inc(cn_hi, 1)
                elif name == "gn_square":
                    act.wait_ge(ke_ok, (b + 1) * TT)
                    act.wait_ge(o_ok, (b + 1) * TT)
                    for h in range(HEADS):
                        nc.scalar.activation(gn_r[:, h, :], o_sb[:, h, :], ACT.Square).then_inc(gn_sq, 1)
                elif name == "gn_sum":
                    for h in range(HEADS):
                        act.wait_ge(gn_sum_pe, b * HEADS + h + 1)
                        nc.scalar.activation(gn_r[:, h, :], acc[:, GN_BANK[h], :], ACT.Ln,
                                             bias=eps_col[:, :]).then_inc(gn_rs, 1)
                elif name == "gn_rstd":
                    for h in range(HEADS):
                        act.wait_ge(gn_rs, b * HEADS * 2 + h + 1)
                        nc.scalar.activation(gn_r[:, h, :], gn_r[:, h, :], ACT.Exp, scale=-0.5).then_inc(gn_rs, 1)
                elif name == "gn_mixed":
                    m, h = b - 1, step[1]
                    for i in trailing(h, HEADS):
                        act.wait_ge(gn_f, m * HEADS + i + 1)
                        nc.scalar.activation(mix_hi[:, i, :], o_sb[:, i, :], ACT.Copy).then_inc(gn_hi, 1)

            for t in range(TT + 1):
                if t < TT:
                    x_sq(0, t)
                if t > 0:
                    xt_hi(0, t - 1)
                    split_hi(t - 1, t - 1, t - 1, -1, t - 1)
            run(act, do)

        @block.vector
        def _(dve):
            dve.wait_ge(g1_ld, 16)

            def carry_wait():
                nc.vector.tensor_copy(pace[:, :], one_col[:, :])

            def tap(m, i):
                a, k = divmod(i, 2 * TAPS)
                k, j = k // 2, 2 * a + k % 2
                if k == 0:
                    dve.wait_ge(u_ok, m * 2 * CT + 2 * j + 2)
                    if not first(m):
                        dve.wait_ge(cn_lo, m * CT - CT + j + 1)
                    nc.vector.tensor_scalar(y_sb[:, j, :], u_sb[:, j, 0:BLK], cw_col[:, j, 0:1],
                                            cb_col[:, j:j + 1], ALU.mult, ALU.add).then_inc(tap_ok, 1)
                else:
                    dve.wait_ge(tap_ok, m * ALL_TAPS + i - 1)
                    nc.vector.scalar_tensor_tensor(out=y_sb[:, j, :], in0=u_sb[:, j, k:k + BLK],
                                                   scalar=cw_col[:, j, k:k + 1], in1=y_sb[:, j, :],
                                                   op0=ALU.mult, op1=ALU.add).then_inc(tap_ok, 1)

            def x_nrm(b, t):
                dve.wait_ge(x_rstd, (b * TT + t + 1) * 3)
                nc.vector.scalar_tensor_tensor(out=x_tile(b, t), in0=x_tile(b, t),
                                               scalar=rstd[:, t:t + 1], in1=g1_row[:, :],
                                               op0=ALU.mult, op1=ALU.mult).then_inc(x_norm, 1)

            def xt_low(b, t):
                for g in range(2):
                    dve.wait_ge(xt_hi_ok, b * 2 * TT + 2 * t + g + 1)
                    src = acc[:, X_BANKS[t][g], :].rearrange("p (k c) -> p k c", c=P)
                    at = (slice(None), slice(g * 4, g * 4 + 4), slice(t * P, (t + 1) * P))
                    nc.vector.tensor_tensor(xT_lo[at], src, xT_hi[at].bitcast(F32), ALU.subtract).then_inc(low_ok, 1)

            def do(step, b):
                name = step[0]
                if name == "conv_in":
                    m, j = b + 1, step[1]
                    if not first(m):
                        dve.wait_ge(tap_ok, m * ALL_TAPS - (0 if j >= 2 else 2 * TAPS))
                    nc.vector.tensor_copy(u_sb[:, j, 0:HALO], u_sb[:, j, BLK:BLK + HALO]).then_inc(u_ok, 1)
                    dve.wait_ge(w_used, base(b) + step[2] + 2)
                    dve.wait_ge(csig_ok, m * CT + j + 1)
                    dve.wait_ge(u_ok, m * 2 * CT + 2 * j + 1)
                    nc.vector.tensor_tensor(u_sb[:, j, HALO:HALO + BLK], acc[:, 1, :], sig[:, j % 2, :],
                                            ALU.mult).then_inc(u_ok, 1)
                elif name == "make_wz":
                    dve.wait_ge(consts_ld, CONSTS)
                    dve.wait_ge(h_st, 16)
                    dve.wait_ge(wz_ok, 1)
                    nc.vector.tensor_tensor(wz[:, :, 1, :], wz_raw[:, :, :], wz[:, :, 0, :].bitcast(F32),
                                            ALU.subtract).then_inc(wz_ok, 1)
                elif name == "taps" or name == "early_taps":
                    for i in range(step[1], step[1] + step[2]):
                        tap(b if name == "taps" else b + 1, i)
                elif name == "gate":
                    j = step[1]
                    dve.wait_ge(gate_act, b * 4 + j + 1)
                    if j == 0 and not first(b):
                        dve.wait_ge(fac_ok, b * TT)
                    nc.vector.tensor_scalar(cum[:, j, :], acc[:, 0, :], bg_col[:, j:j + 1], 0.0,
                                            ALU.add, ALU.min).then_inc(gate_min, 1)
                elif name == "decay":
                    dve.wait_ge(gate_act, b * 4 + 4)
                    dve.wait_ge(gate_min, (b + 1) * PAIRS)
                    for j in range(PAIRS):
                        for c in range(TT):
                            t = slice(c * P, (c + 1) * P)
                            nc.vector.tensor_tensor_scan(cum[:, j, t], cum[:, j, t], log1p_t[:, j, t], 0.0,
                                                         ALU.add, ALU.subtract).then_inc(cum_ok, 1)
                elif name == "g":
                    j = step[1]
                    dve.wait_ge(gsig_ok, b * HEADS + j + 1)
                    if j == 0 and not first(b):
                        dve.wait_ge(gn_f, b * HEADS)
                    nc.vector.tensor_tensor(silu_g[:, j, :], acc[:, G_BANK[j], :], sig[:, j % 2, :],
                                            ALU.mult).then_inc(silu_ok, 1)
                elif name == "x_norm":
                    x_nrm(b + 1, step[1])
                elif name == "x_tr":
                    xt_low(b + 1, step[1])
                elif name == "out_done":
                    half, m = step[1], b - 1
                    dve.wait_ge(res_ld[half], (m + 1) * 16)
                    rows = res(m, half)
                    for t in range(TT):
                        if t < TT - 1:
                            dve.wait_ge(out_pe, (m * 2 + half) * (TT - 1) + t + 1)
                        else:
                            dve.wait_ge(w_used, base(b) + step[2] + 1)
                        nc.vector.tensor_tensor(rows[:, t, :], acc[:, out_bank(b, half, t), :], rows[:, t, :],
                                                ALU.add).then_inc(sum_ok, 1)
                elif name == "gla_expo":
                    c = step[1]
                    if c == 0:
                        dve.wait_ge(cum_ok, (b + 1) * 2 * TT)
                        if not first(b):
                            dve.wait_ge(gn_n, b * HEADS)
                    if c > 0 or not first(b):
                        dve.wait_ge(ke_ok, b * TT + c)
                    cc = cum[:, :, c * P:(c + 1) * P]
                    for lv, s in enumerate(LEVELS):
                        n = P // (2 * s)
                        c5 = cc.rearrange("p a (n h s) -> p a n h s", h=2, s=s)
                        f5 = fac[:, lv, :, :].rearrange("p a (n h s) -> p a n h s", h=2, s=s)
                        ref = c5[:, :, :, 0, s - 1:s].broadcast_to([P, PAIRS, n, s])
                        nc.vector.tensor_tensor(f5[:, :, :, 0, :], ref, c5[:, :, :, 0, :], ALU.subtract)
                        nc.vector.tensor_tensor(f5[:, :, :, 1, :], c5[:, :, :, 1, :], ref, ALU.subtract)
                    nc.vector.tensor_tensor(fac[:, NL, :, :], cc[:, :, P - 1:P].broadcast_to([P, PAIRS, P]), cc,
                                            ALU.subtract).then_inc(expo_ok, 1)
                elif name == "gla_select":
                    c, a = step[1:]
                    dve.wait_ge(score_pe, (b * TT + c) * PAIRS + a + 1)
                    if c > 0 or not first(b):
                        dve.wait_ge(o_pe, b * TT + c)
                    n0 = ((b * TT + c) * PAIRS + a) * (NL + 1)
                    carry_wait()
                    hh = slice(2 * a, 2 * a + 2)
                    diag = acc[:, 3, DIAG:DIAG + 2].unsqueeze(2).broadcast_to([P, 2, P])
                    nc.vector.copy_predicated(probs[:, hh, :], ident[:, :].bitcast(I32).unsqueeze(1).broadcast_to([P, 2, P]),
                                              diag).then_inc(probs_ok, 1)
                    for lv, s in enumerate(LEVELS):
                        n = P // (2 * s)
                        dve.wait_ge(probs_ok, n0 + lv + 1)
                        carry_wait()
                        dst = probs[:, hh, :].rearrange("p a (n h s) -> p a n h s", h=2, s=s)[:, :, :, 1, :]
                        src = acc[:, 2 + lv // 4, lv % 4 * P:lv % 4 * P + P].rearrange("p (a n s) -> p a n s", a=2, s=s)
                        msk = lvl_mask[:, lv, :].bitcast(I32).rearrange("p (n s) -> p n s", s=s)
                        nc.vector.copy_predicated(dst, msk.unsqueeze(1).broadcast_to([P, 2, n, s]),
                                                  src).then_inc(probs_ok, 1)
                elif name == "gla_out":
                    c = step[1]
                    dve.wait_ge(upd_pe, b * TT + c + 1)
                    if c > 0 or not first(b):
                        dve.wait_ge(state_ok, (b * TT + c) * HEADS)
                    for h in range(HEADS):
                        a, r = h // 2, slice(h % 2 * DK, h % 2 * DK + DK)
                        nc.vector.scalar_tensor_tensor(out=state[r, h, :], in0=state[r, h, :],
                                                       scalar=decay[r, c % 2, a:a + 1],
                                                       in1=acc[r, 7, KEY + a * DV:KEY + (a + 1) * DV],
                                                       op0=ALU.mult, op1=ALU.add).then_inc(state_ok, 1)
                elif name == "cn_mean":
                    for j in pair(step):
                        dve.wait_ge(cn_mean_pe, b * CT + j + 1)
                        nc.vector.tensor_tensor(y_sb[:, j, :], y_sb[:, j, :], acc[:, CN_BANK[j], :],
                                                ALU.subtract).then_inc(cn_dev, 1)
                elif name == "cn_rstd" and isinstance(b, int) and b == NB - 1:
                    for j in range(CT):
                        dve.wait_ge(cn_rs, b * CT * 2 + CT + j + 1)
                        nc.vector.tensor_tensor(y_sb[:, j, :], y_sb[:, j, :], nr[:, j, :], ALU.mult).then_inc(cn_n, 1)
                elif name == "cn_mixed":
                    j = step[1]
                    dve.wait_ge(cn_sig, b * CT + j + 1)
                    nc.vector.tensor_scalar(y_sb[:, j, :], y_sb[:, j, :], cg_col[:, j:j + 1], cnb_col[:, j:j + 1],
                                            ALU.mult, ALU.add).then_inc(cn_aff, 1)
                    if isinstance(b, int) and b == NB - 1:
                        dve.wait_ge(cn_aff, b * CT + j + 1)
                        nc.vector.tensor_tensor(y_sb[:, j, :], y_sb[:, j, :], nr[:, j, :], ALU.mult).then_inc(cn_f, 1)
                        for i in trailing(j, CT):
                            dve.wait_ge(cn_hi, b * CT + i + 1)
                            nc.vector.tensor_tensor(mix_lo[:, HEADS + i, :], y_sb[:, i, :],
                                                    mix_hi[:, HEADS + i, :].bitcast(F32), ALU.subtract).then_inc(cn_lo, 1)
                elif name == "gn_rstd":
                    for h in range(HEADS):
                        dve.wait_ge(gn_rs, b * HEADS * 2 + HEADS + h + 1)
                        nc.vector.scalar_tensor_tensor(out=o_sb[:, h, :], in0=o_sb[:, h, :], scalar=gn_col[:, 0:1],
                                                       in1=gn_r[:, h, :], op0=ALU.mult, op1=ALU.mult).then_inc(gn_n, 1)

            for t in range(TT + 1):
                if t < TT:
                    x_nrm(0, t)
                if t > 0:
                    xt_low(0, t - 1)
            dve.wait_ge(made, MADE)
            run(dve, do)

        @block.tensor
        def _(pe):
            pe.wait_ge(made, MADE_IDENT)

            def x_tr(b, t):
                pe.wait_ge(x_norm, b * TT + t + 1)
                free_banks_x(b, t)
                for g in range(2):
                    bank = X_BANKS[t][g]
                    for k in range(4):
                        kk = g * 4 + k
                        ins = nc.tensor.transpose(acc[:, bank, k * P:(k + 1) * P],
                                                  x_tile(b, t)[:, kk * P:(kk + 1) * P], ident[:, :])
                    ins.then_inc(xt_pe, 1)

            def free_banks_x(m, t):
                if t < 2:
                    if not first(m):
                        pe.wait_ge(*((v_ok, m * TT) if t == 0 else (silu_ok, m * HEADS)))
                elif isinstance(m, int) and m < 2:
                    pe.wait_ge(low_ok, m * LOWS + (4 if t == 2 else 2))
                else:
                    pe.wait_ge(sum_ok, (m - 1) * LOWS - TT)

            def weights(b, i):
                pe.wait_ge(w_lo_ok, base(b) + i + 1)

            def column_tile(step, b, bank):
                for i in range(2):
                    n = step[2] + i
                    weights(b, n)
                    for k in range(4):
                        kk = i * 4 + k
                        c = slice(k * P, (k + 1) * P)
                        ins = three_products(nc, acc[:, bank, :], w_hi[:, n % SLOTS, c], w_lo[:, n % SLOTS, c],
                                             xT_hi[:, kk, :], xT_lo[:, kk, :], kk == 0, kk == KT - 1)
                    ins.then_inc(w_used, 1)

            def do(step, b):
                name = step[0]
                if name == "conv_gate":
                    m, j = b + 1, step[1]
                    if j == 0:
                        pe.wait_ge(low_ok, (m + 1) * LOWS)
                        if not first(b):
                            pe.wait_ge(sum_ok, b * LOWS - TT + 1)
                    else:
                        pe.wait_ge(csig_ok, m * CT + j)
                    column_tile(step, b, 0)
                elif name == "conv_in":
                    m, j = b + 1, step[1]
                    if j > 0:
                        pe.wait_ge(u_ok, m * 2 * CT + 2 * j)
                    elif not first(b):
                        pe.wait_ge(sum_ok, b * LOWS - TT + 2)
                    column_tile(step, b, 1)
                elif name == "z":
                    pe.wait_ge(csig_ok, (b + 1) * CT)
                    if first(b):
                        pe.wait_ge(wz_ok, 2)
                        pe.wait_ge(consts_ld, CONSTS)
                        pe.wait_ge(made, MADE)
                    for k in range(KT):
                        w = wz[:, k, :, :].rearrange("p a r -> p (a r)")
                        nc.tensor.matmul(acc[0:2 * RANK, 0, :], w, xT_hi[:, k, :], start=(k == 0), stop=False)
                        ins = nc.tensor.matmul(acc[0:2 * RANK, 0, :], w, xT_lo[:, k, :], start=False, stop=(k == KT - 1))
                    ins.then_inc(z_pe, 1)
                elif name == "gate":
                    j = step[1]
                    if j == 0:
                        pe.wait_ge(z_ok, b + 1)
                    else:
                        pe.wait_ge(gate_min, b * PAIRS + j)
                    nc.tensor.matmul(acc[:, 0, :], w_up[:, j * P:(j + 1) * P], z_sb, start=True,
                                     stop=True).then_inc(gate_pe, 1)
                elif name == "qk":
                    j = step[1]
                    if j == 0:
                        pe.wait_ge(u_ok, (b + 1) * 2 * CT)
                    elif j < 3:
                        pe.wait_ge(qk_ok, b * 4 + j)
                    else:
                        pe.wait_ge(gate_min, (b + 1) * PAIRS)
                    column_tile(step, b, QK_BANK[j])
                elif name == "v":
                    k = step[1]
                    if k == 0:
                        pe.wait_ge(qk_ok, b * 4 + 4)
                        if not first(b):
                            pe.wait_ge(cn_rs, b * CT * 2)
                    weights(b, step[2])
                    slot = step[2] % SLOTS
                    for t in range(TT):
                        c = slice(t * P, (t + 1) * P)
                        out = acc[:, V_BANK[t], :]
                        nc.tensor.matmul(out, xT_hi[:, k, c], w_hi[:, slot, :], start=(k == 0), stop=False)
                        nc.tensor.matmul(out, xT_hi[:, k, c], w_lo[:, slot, :], start=False, stop=False)
                        ins = nc.tensor.matmul(out, xT_lo[:, k, c], w_hi[:, slot, :], start=False, stop=(k == KT - 1))
                        if t == TT - 1:
                            ins.then_inc(w_used, 1)
                        elif k == KT - 1:
                            ins.then_inc(v_pe, 1)
                elif name == "g":
                    j = step[1]
                    if j < 2:
                        pe.wait_ge(v_ok, b * TT + j + 1)
                    else:
                        pe.wait_ge(silu_ok, b * HEADS + j - 1)
                    column_tile(step, b, G_BANK[j])
                elif name == "x_tr":
                    x_tr(b + 1, step[1])
                elif name == "out":
                    (half, k), m = step[1], b - 1
                    if half == 0 and k < HEADS:
                        pe.wait_ge(gn_lo, (b - 1) * HEADS + k + 1)
                    elif half == 0:
                        pe.wait_ge(cn_lo, (b - 1) * CT + k - HEADS + 1)
                    if k == 0:
                        if isinstance(b, int) and b == NB - 1:
                            if half == 0:
                                pe.wait_ge(v_ok, (b + 1) * TT)
                                pe.wait_ge(silu_ok, (b + 1) * HEADS)
                        elif not isinstance(b, int):
                            pe.wait_ge(low_ok, (b + 1) * LOWS + half * TT + 2)
                        elif half == 0:
                            pe.wait_ge(sum_ok, m * LOWS)
                            pe.wait_ge(gn_rs, b * HEADS * 2)
                        else:
                            pe.wait_ge(cn_rs, b * CT * 2 - CT)
                    weights(b, step[2])
                    slot = step[2] % SLOTS
                    for t in range(TT):
                        c = slice(t * P, (t + 1) * P)
                        out = acc[:, out_bank(b, half, t), :]
                        if k == 0 and t == 2 and not isinstance(b, int):
                            pe.wait_ge(low_ok, (b + 1) * LOWS + (half + 1) * TT)
                        elif k == 0 and isinstance(b, int) and b < NB and half == 1:
                            pe.wait_ge(sum_ok, m * LOWS + OUT_BANK[0].index(OUT_BANK[1][t]) + 1)
                        nc.tensor.matmul(out, mix_hi[:, k, c], w_hi[:, slot, :], start=(k == 0), stop=False)
                        nc.tensor.matmul(out, mix_hi[:, k, c], w_lo[:, slot, :], start=False, stop=False)
                        ins = nc.tensor.matmul(out, mix_lo[:, k, c], w_hi[:, slot, :], start=False, stop=(k == KT - 1))
                        if t == TT - 1:
                            ins.then_inc(w_used, 1)
                        elif k == KT - 1:
                            ins.then_inc(out_pe, 1)
                elif name == "cn_mean":
                    pe.wait_ge(tap_ok, b * ALL_TAPS + (step[1] + 1) * 2 * TAPS)
                    if step[1] > 0:
                        pe.wait_ge(cn_dev, b * CT + 2)
                    elif not first(b):
                        pe.wait_ge(sum_ok, b * LOWS)
                    for j in pair(step):
                        nc.tensor.matmul(acc[:, CN_BANK[j], :], mean_grp[:, :], y_sb[:, j, :], start=True,
                                         stop=True).then_inc(cn_mean_pe, 1)
                elif name == "cn_var":
                    if step[1] > 0:
                        pe.wait_ge(cn_rs, b * CT * 2 + 2)
                    else:
                        pe.wait_ge(cn_dev, (b + 1) * CT)
                    for j in pair(step):
                        pe.wait_ge(cn_sq, b * CT + j + 1)
                        nc.tensor.matmul(acc[:, CN_BANK[j], :], mean_grp[:, :], nr[:, j, :], start=True,
                                         stop=True).then_inc(cn_var_pe, 1)
                elif name == "gla_scores":
                    c, a = step[1:]
                    if a == 0:
                        pe.wait_ge(qe_ok, (b * TT + c + 1) * 2)
                    if c == 0 and a == 0:
                        if not first(b):
                            pe.wait_ge(gn_rs, b * HEADS * 2)
                    else:
                        pe.wait_ge(probs_ok, ((b * TT + c) * PAIRS + a) * (NL + 1))
                    for lv in range(NL):
                        out = acc[:, 2 + lv // 4, lv % 4 * P:lv % 4 * P + P]
                        nc.tensor.matmul(out, ke[:, lv, a, :], qe_head[:, lv, a, :, :].rearrange("p h c -> p (h c)"),
                                         start=True, stop=True)
                    ins = nc.tensor.matmul(acc[:, 3, DIAG:DIAG + 2], qk[:, a, :], head_cols[:, :], start=True, stop=True)
                    ins.then_inc(score_pe, 1)
                    if a == 0:
                        if c > 0 or not first(b):
                            pe.wait_ge(state_ok, (b * TT + c) * HEADS)
                            pe.wait_ge(kT_ok, b * TT + c)
                        for i in range(PAIRS):
                            ins = nc.tensor.transpose(acc[:, 7, i * P:(i + 1) * P], k_end[:, i, :], ident[:, :])
                        ins.then_inc(kT_pe, 1)
                elif name == "gla_out":
                    c = step[1]
                    if c == 0:
                        pe.wait_ge(v_ok, (b + 1) * TT)
                    if c > 0 or not first(b):
                        pe.wait_ge(o_ok, b * TT + c)
                    pe.wait_ge(probs_ok, (b * TT + c + 1) * PAIRS * (NL + 1))
                    for h in range(HEADS):
                        a = h // 2
                        out = acc[:, 6, h * P:(h + 1) * P]
                        nc.tensor.matmul(out, state[:, h, :], q_in[:, c % 2, a, :], start=True, stop=False)
                        ins = nc.tensor.matmul(out, v_sb[:, c, h * DV:(h + 1) * DV], probs[:, h, :],
                                               start=False, stop=True)
                    ins.then_inc(o_pe, 1)
                    pe.wait_ge(kT_ok, b * TT + c + 1)
                    for h in range(HEADS):
                        a, r = h // 2, slice(h % 2 * DK, h % 2 * DK + DK)
                        ins = nc.tensor.matmul(acc[r, 7, KEY + a * DV:KEY + (a + 1) * DV], k_endT[:, a, r],
                                               v_sb[:, c, h * DV:(h + 1) * DV], start=True, stop=True)
                    ins.then_inc(upd_pe, 1)
                elif name == "gn_sum":
                    pe.wait_ge(o_ok, (b + 1) * TT)
                    pe.wait_ge(state_ok, (b + 1) * TT * HEADS)
                    for h in range(HEADS):
                        pe.wait_ge(gn_sq, b * HEADS + h + 1)
                        nc.tensor.matmul(acc[:, GN_BANK[h], :], mean_dv[:, :], gn_r[:, h, :], start=True,
                                         stop=True).then_inc(gn_sum_pe, 1)

            for t in range(TT):
                x_tr(0, t)
            run(pe, do)


CONSTS = 16 * (1 + 2 + 4 + 1)
MADE_IDENT = 5
MADE = 16 + P // CONV_GROUP + 1 + 2 * NL
QK_BANK = [1, 1, 1, 0]
G_BANK = [1, 0, 1, 0]
X_BANKS = [(4, 5), (0, 1), (0, 1), (4, 5)]
OUT_BANK = [(4, 5, 0, 1), (0, 1, 4, 5)]
LAST_OUT_BANK = [(0, 1, 2, 3), (6, 7, 4, 5)]
V_BANK = [1, 0, 4, 5]
GN_BANK = [2, 3, 6, 7]
DIAG = (NL - 4) * P
CN_BANK = [4, 5, 4, 5]


def mlp_block(nc, h_dram, h_st, norm2_g, w_mlp_in, w_mlp_out, final_norm_g, out):
    with ExitStack() as ctx:
        def sb(name, shape, dt=F32):
            return ctx.enter_context(nc.sbuf_tensor(name, shape, dt))

        def sem(name):
            return ctx.enter_context(nc.semaphore(name))

        h_sb = sb("h_sb", [P, HT, D_MODEL])
        hn = sb("hn", [P, HN, D_MODEL])
        m_junk = sb("m_junk", [P, D_MODEL], BF16)
        g2_row = sb("g2_row", [P, D_MODEL])
        gf_row = sb("gf_row", [P, D_MODEL])
        m_ssq = sb("m_ssq", [P, 2 * NH * HT])
        m_rstd = sb("m_rstd", [P, 2 * NH * HT])
        m_neg_half = sb("m_neg_half", [P, 1])
        m_eps = sb("m_eps", [P, 1])
        m_inv_d = sb("m_inv_d", [P, 1])
        m_ident = sb("m_ident", [P, P])
        hT_hi = sb("hT_hi", [P, KT, HALF], F32R)
        hT_lo = sb("hT_lo", [P, KT, HALF], F32R)
        raw = sb("raw", [P, 2 * FT, D_MODEL])
        m_hi = sb("m_hi", [P, 2 * FT, D_MODEL], F32R)
        m_lo = sb("m_lo", [P, 2 * FT, D_MODEL], F32R)
        relu = sb("relu", [P, 2 * FT, 512])
        ff_hi = sb("ff_hi", [P, FT, HALF], F32R)
        ff_lo = sb("ff_lo", [P, FT, HALF], F32R)
        ps = ctx.enter_context(nc.psum_tensor("ps", [P, 8, 512], F32))

        g2_ld = sem("g2_ld")
        gf_ld = sem("gf_ld")
        m_made = sem("m_made")
        hn_ld = [sem(f"hn_ld{i}") for i in range(HN)]
        h_ld = [sem(f"h_ld{i}") for i in range(HT)]
        out_st = [sem(f"out_st{i}") for i in range(HT)]
        m_ld = [sem(f"m_ld{i}") for i in range(2 * FT)]
        sq_ok = sem("sq_ok")
        rs_ok = sem("rs_ok")
        hn_ok = sem("hn_ok")
        tr_pe = sem("tr_pe")
        tr_hi_ok = sem("tr_hi_ok")
        tr_lo_ok = sem("tr_lo_ok")
        m_hi_ok = sem("m_hi_ok")
        m_lo_ok = sem("m_lo_ok")
        up_pe = sem("up_pe")
        relu_ok = sem("relu_ok")
        sqr_ok = sem("sqr_ok")
        ff_hi_ok = sem("ff_hi_ok")
        ff_lo_ok = sem("ff_lo_ok")
        down_pe = sem("down_pe")
        add_ok = sem("add_ok")
        fin_ok = sem("fin_ok")
        block = ctx.enter_context(nc.Block())

        NG = HT * 2
        UP = 2 * FT

        def run(eng, begin, step):
            begin()
            for half in range(NH):
                step(half * NF)
                with eng.Fori(half * NF + 1, (half + 1) * NF - 1) as f:
                    step(f)
                step((half + 1) * NF - 1)

        def wait(eng, sem_, count):
            if not (isinstance(count, int) and count <= 0):
                eng.wait_ge(sem_, count)

        def is_step(f, n):
            return isinstance(f, int) and f == n

        h_t = h_dram.rearrange("(n p) d -> p n d", p=P)
        out_t = out.rearrange("(n p) d -> p n d", p=P)
        w1_t = w_mlp_in.rearrange("(k p) f -> p k f", p=P)
        w2_t = w_mlp_out.rearrange("(f p) d -> p f d", p=P)

        @block.sync
        def _(sp):
            def hn_load(n):
                if n >= HN:
                    sp.wait_ge(tr_pe, 2 * (n - HN + 1))
                sp.dma_start(hn[:, n % HN, :], h_t[:, n, :]).then_inc(hn_ld[n % HN], 16)

            def h_load(half, t):
                if half > 0:
                    sp.wait_ge(out_st[t], half * 16)
                sp.dma_start(h_sb[:, t, :], h_t[:, half * HT + t, :]).then_inc(h_ld[t], 16)

            def out_store(half, t):
                sp.wait_ge(fin_ok, half * HT + t + 1)
                sp.dma_start(out_t[:, half * HT + t, :], h_sb[:, t, :]).then_inc(out_st[t], 16)

            def weights(f, g):
                for i in range(2 * FT):
                    wait(sp, m_lo_ok, (f - 1) * 2 * FT + i + 1)
                    if i < FT:
                        src = w1_t[:, :, bass.ds(g * FC + i * P, P)]
                        dst = raw[:, i, :].rearrange("p (k c) -> p k c", c=P)
                    else:
                        src = w2_t[:, bass.ds(g * FT + i - FT, 1), :].rearrange("p a d -> p (a d)")
                        dst = raw[:, i, :]
                    sp.dma_start(dst, src).then_inc(m_ld[i], 16)

            sp.wait_ge(h_st, (NB * 2 - 1) * 16)
            sp.dma_start(hn[:, 0, :], h_t[:, 0, :]).then_inc(hn_ld[0], 16)
            sp.dma_start(g2_row[:, :], norm2_g.partition_broadcast(P)).then_inc(g2_ld, 16)
            for n in range(1, HN):
                hn_load(n)
            weights(0, 0)
            for n in range(HN, HT):
                hn_load(n)
            for t in range(HT):
                h_load(0, t)
            sp.dma_start(gf_row[:, :], final_norm_g.partition_broadcast(P)).then_inc(gf_ld, 16)
            for half in range(NH):
                if half > 0:
                    for t in range(HT):
                        out_store(half - 1, t)
                    for t in range(HT):
                        h_load(half, t)
                with sp.Fori(1, NF) as g:
                    weights(g + half * NF, g)
                if half + 1 < NH:
                    sp.wait_ge(h_st, (NB * 2 + 1) * 16)
                    for n in range((half + 1) * HT, (half + 1) * HT + HN):
                        hn_load(n)
                    weights((half + 1) * NF, 0)
                    for n in range((half + 1) * HT + HN, (half + 2) * HT):
                        hn_load(n)
            for t in range(HT):
                out_store(NH - 1, t)
            for t in range(HT):
                sp.wait_ge(out_st[t], NH * 16)

        @block.gpsimd
        def _(pool):
            nc.gpsimd.memset(m_neg_half[:, :], -0.5)
            nc.gpsimd.memset(m_eps[:, :], EPS)
            nc.gpsimd.memset(m_inv_d[:, :], 1.0 / D_MODEL)
            nc.gpsimd.memset(m_ident[:, :], 0.0).then_inc(m_made, 1)
            pool.wait_ge(m_made, 1)
            nc.gpsimd.affine_select(out=m_ident[:, :], in_=m_ident[:, :], compare_op=ALU.not_equal, fill=1.0,
                                    base=0, pattern=[[-1, P]], channel_multiplier=1).then_inc(m_made, 1)

            def row_rstd(n):
                pool.wait_ge(sq_ok, n + 1)
                for i, (a, const, op) in enumerate(((m_ssq, m_inv_d, ALU.mult), (m_rstd, m_eps, ALU.add),
                                                    (m_rstd, m_neg_half, ALU.pow))):
                    if i > 0:
                        pool.wait_ge(rs_ok, 3 * n + i)
                    nc.gpsimd.tensor_tensor(m_rstd[:, n:n + 1], a[:, n:n + 1], const[:, :], op).then_inc(rs_ok, 1)

            def low(f, i):
                pool.wait_ge(m_hi_ok, f * 2 * FT + i + 1)
                nc.gpsimd.tensor_tensor(m_lo[:, i, :], raw[:, i, :], m_hi[:, i, :].bitcast(F32),
                                        ALU.subtract).then_inc(m_lo_ok, 1)

            def step(f):
                for i in range(2 * FT):
                    if not (is_step(f, NF) and i < FT):
                        low(f, i)
                if is_step(f, NF - 1):
                    for n in range(HT, HT + HN):
                        row_rstd(n)
                    for i in range(FT):
                        low(NF, i)
                    for n in range(HT + HN, 2 * HT):
                        row_rstd(n)
                if is_step(f, NF) or is_step(f, 2 * NF - 1):
                    for t in range(HT):
                        row_rstd((2 if f == NF else 3) * HT + t)

            def begin():
                for n in range(HT):
                    row_rstd(n)

            run(pool, begin, step)

        @block.scalar
        def _(act):
            def square(n):
                act.wait_ge(hn_ld[n % HN], (n // HN + 1) * 16)
                wait(act, sq_ok, n)
                nc.scalar.activation(m_junk[:, :], hn[:, n % HN, :], ACT.Square,
                                     accum_out=m_ssq[:, n:n + 1]).then_inc(sq_ok, 1)

            def transposed_hi(n):
                half, t = divmod(n, HT)
                for g in range(2):
                    i = 2 * n + g
                    act.wait_ge(tr_pe, i + 1)
                    nc.scalar.activation(hT_hi[:, g * 4:g * 4 + 4, t * P:(t + 1) * P],
                                         ps[:, i % 4, :].rearrange("p (k c) -> p k c", c=P),
                                         ACT.Copy).then_inc(tr_hi_ok, 1)

            def last_square(half, t):
                n = (half + 2) * HT + t
                act.wait_ge(add_ok, ((half + 1) * NF - 1) * NG + 2 * t + 2)
                act.wait_ge(sq_ok, n)
                nc.scalar.activation(m_junk[:, :], h_sb[:, t, :], ACT.Square,
                                     accum_out=m_ssq[:, n:n + 1]).then_inc(sq_ok, 1)

            def split_hi(f, i):
                act.wait_ge(m_ld[i], (f + 1) * 16)
                if i < FT:
                    wait(act, up_pe, f * UP)
                else:
                    wait(act, down_pe, f * NG)
                nc.scalar.activation(m_hi[:, i, :], raw[:, i, :], ACT.Copy).then_inc(m_hi_ok, 1)

            def ff(f, i):
                act.wait_ge(up_pe, f * UP + i + 1)
                if i == 0:
                    wait(act, ff_lo_ok, f * UP)
                nc.scalar.activation(relu[:, i, :], ps[:, i, :], ACT.Relu).then_inc(relu_ok, 1)
                t, q = i // 2, i % 2
                act.wait_ge(sqr_ok, f * UP + i + 1)
                nc.scalar.activation(ff_hi[:, t, q * 512:(q + 1) * 512], relu[:, i, :], ACT.Copy).then_inc(ff_hi_ok, 1)

            def step(f):
                for i in range(2 * FT):
                    if not (is_step(f, NF) and i < FT):
                        split_hi(f, i)
                for i in range(UP):
                    if is_step(f, NF - 1):
                        square(HT + i)
                    if is_step(f, NF):
                        last_square(0, 2 * i)
                        last_square(0, 2 * i + 1)
                    ff(f, i)
                if is_step(f, NF - 1):
                    for i in range(FT):
                        split_hi(NF, i)
                    for n in range(HT, 2 * HT):
                        transposed_hi(n)
                        if n + HN < 2 * HT:
                            square(n + HN)
                if is_step(f, 2 * NF - 1):
                    for t in range(HT):
                        last_square(1, t)

            def begin():
                for t in range(HT + 1):
                    if t < HT:
                        square(t)
                    if t > 0:
                        transposed_hi(t - 1)

            run(act, begin, step)

        @block.vector
        def _(dve):
            def normalise(n):
                dve.wait_ge(rs_ok, 3 * (n + 1))
                nc.vector.scalar_tensor_tensor(out=hn[:, n % HN, :], in0=hn[:, n % HN, :], scalar=m_rstd[:, n:n + 1],
                                               in1=g2_row[:, :], op0=ALU.mult, op1=ALU.mult).then_inc(hn_ok, 1)

            def transposed_lo(n):
                half, t = divmod(n, HT)
                for g in range(2):
                    i = 2 * n + g
                    dve.wait_ge(tr_hi_ok, i + 1)
                    at = (slice(None), slice(g * 4, g * 4 + 4), slice(t * P, (t + 1) * P))
                    nc.vector.tensor_tensor(hT_lo[at], ps[:, i % 4, :].rearrange("p (k c) -> p k c", c=P),
                                            hT_hi[at].bitcast(F32), ALU.subtract).then_inc(tr_lo_ok, 1)

            def last_norm(half, t):
                n = (half + 2) * HT + t
                dve.wait_ge(rs_ok, 3 * (n + 1))
                nc.vector.scalar_tensor_tensor(out=h_sb[:, t, :], in0=h_sb[:, t, :], scalar=m_rstd[:, n:n + 1],
                                               in1=gf_row[:, :], op0=ALU.mult, op1=ALU.mult).then_inc(fin_ok, 1)

            def step(f):
                for i in range(UP):
                    if is_step(f, NF):
                        last_norm(0, 2 * i)
                        last_norm(0, 2 * i + 1)
                    dve.wait_ge(relu_ok, f * UP + i + 1)
                    nc.vector.tensor_tensor(relu[:, i, :], relu[:, i, :], relu[:, i, :], ALU.mult).then_inc(sqr_ok, 1)
                    dve.wait_ge(ff_hi_ok, f * UP + i + 1)
                    t, c = i // 2, slice(i % 2 * 512, i % 2 * 512 + 512)
                    nc.vector.tensor_tensor(ff_lo[:, t, c], relu[:, i, :], ff_hi[:, t, c].bitcast(F32),
                                            ALU.subtract).then_inc(ff_lo_ok, 1)
                if is_step(f, NF - 1):
                    for n in range(HT, HT + 2):
                        normalise(n)
                for n in range(NG):
                    t, c = n // 2, slice(n % 2 * 512, n % 2 * 512 + 512)
                    if n % 2 == 0 and isinstance(f, int) and f % NF == 0:
                        dve.wait_ge(h_ld[t], (f // NF + 1) * 16)
                    dve.wait_ge(down_pe, f * NG + n + 1)
                    nc.vector.tensor_tensor(h_sb[:, t, c], ps[:, 4 + n % 4, :], h_sb[:, t, c],
                                            ALU.add).then_inc(add_ok, 1)
                    if n % 2 == 1 and is_step(f, NF - 1):
                        transposed_lo(HT + t)
                        if t + 2 < HT:
                            normalise(HT + t + 2)
                    if n % 2 == 1 and is_step(f, 2 * NF - 1) and t > 1:
                        last_norm(1, t - 2)
                if is_step(f, 2 * NF - 1):
                    last_norm(1, HT - 2)
                    last_norm(1, HT - 1)

            def begin():
                dve.wait_ge(g2_ld, 16)
                for t in range(HT + 1):
                    if t < HT:
                        normalise(t)
                    if t > 0:
                        transposed_lo(t - 1)
                dve.wait_ge(gf_ld, 16)

            run(dve, begin, step)

        @block.tensor
        def _(pe):
            def transpose(n):
                pe.wait_ge(hn_ok, n + 1)
                for g in range(2):
                    i = 2 * n + g
                    if HT <= n < HT + 2:
                        pe.wait_ge(relu_ok, NF * UP)
                    elif i >= 4:
                        pe.wait_ge(tr_lo_ok, i - 3)
                    for k in range(4):
                        kk = g * 4 + k
                        ins = nc.tensor.transpose(ps[:, i % 4, k * P:(k + 1) * P], hn[:, n % HN, kk * P:(kk + 1) * P],
                                                  m_ident[:, :])
                    ins.then_inc(tr_pe, 1)

            def up(f, i):
                t, q = i // 2, i % 2
                if q == 0:
                    pe.wait_ge(m_lo_ok, f * 2 * FT + t + 1)
                wait(pe, relu_ok, (f - 1) * UP + i + 1)
                for k in range(KT):
                    c = slice(k * P, (k + 1) * P)
                    ins = three_products(nc, ps[:, i, :], m_hi[:, t, c], m_lo[:, t, c],
                                         hT_hi[:, k, q * 512:(q + 1) * 512], hT_lo[:, k, q * 512:(q + 1) * 512],
                                         k == 0, k == KT - 1)
                ins.then_inc(up_pe, 1)

            def down(f, n):
                t, q = n // 2, n % 2
                c = slice(q * 512, (q + 1) * 512)
                r = slice(t * P, (t + 1) * P)
                if n == 0:
                    pe.wait_ge(ff_lo_ok, f * UP + 3)
                if n == NG // 2:
                    pe.wait_ge(ff_lo_ok, f * UP + 4)
                wait(pe, add_ok, f * NG + n - 3)
                for i in range(FT):
                    o = ps[:, 4 + n % 4, :]
                    nc.tensor.matmul(o, ff_hi[:, i, r], m_hi[:, FT + i, c], start=(i == 0), stop=False)
                    nc.tensor.matmul(o, ff_hi[:, i, r], m_lo[:, FT + i, c], start=False, stop=False)
                    ins = nc.tensor.matmul(o, ff_lo[:, i, r], m_hi[:, FT + i, c], start=False, stop=(i == FT - 1))
                ins.then_inc(down_pe, 1)

            def step(f):
                if isinstance(f, int) and f % NF == 0:
                    pe.wait_ge(tr_lo_ok, (f // NF + 1) * 2 * HT)
                for i in range(UP):
                    up(f, i)
                pe.wait_ge(m_lo_ok, (f + 1) * 2 * FT)
                for n in range(NG):
                    down(f, n)
                    if n % 2 == 1 and is_step(f, NF - 1):
                        transpose(HT + n // 2)

            def begin():
                pe.wait_ge(m_made, 2)
                for n in range(HT):
                    transpose(n)

            run(pe, begin, step)


def hybrid_block(nc, x, norm1_g, w_in, w_gate_up, b_gate, gla_norm_g, conv_w, conv_b, conv_norm_g,
                 conv_norm_b, w_out, norm2_g, w_mlp_in, w_mlp_out, final_norm_g, out):
    with ExitStack() as ctx:
        h_dram = nc.dram_tensor("h_dram", [SEQ, D_MODEL], F32).ap()
        h_st = ctx.enter_context(nc.semaphore("h_st"))
        mixer_block(nc, x, norm1_g, w_in, w_gate_up, b_gate, gla_norm_g, conv_w, conv_b, conv_norm_g,
                    conv_norm_b, w_out, h_dram, h_st)
        mlp_block(nc, h_dram, h_st, norm2_g, w_mlp_in, w_mlp_out, final_norm_g, out)


_INS = ["x", "norm1_g", "w_in", "w_gate_up", "b_gate", "gla_norm_g", "conv_w", "conv_b", "conv_norm_g",
        "conv_norm_b", "w_out", "norm2_g", "w_mlp_in", "w_mlp_out", "final_norm_g"]


_PER_CHANNEL = ["b_gate", "gla_norm_g", "conv_w", "conv_b", "conv_norm_g", "conv_norm_b"]


def kernel(**inputs):
    import numpy as np
    import concourse.bacc as bacc
    from concourse.bass_utils import run_bass_kernel_spmd

    nc = bacc.Bacc("TRN2", target_bir_lowering=False, num_devices=1)
    arrays, args = {}, []
    for name in _INS:
        a = np.ascontiguousarray(inputs[name])
        if name != "final_norm_g":
            a = a.reshape(a.shape[1:])
        if name in _PER_CHANNEL:
            a = a.reshape(a.shape[:-1] + (-1, P))
            a = np.ascontiguousarray(np.moveaxis(a, (-1, -2), (0, 1)))
        arrays[f"in_{name}"] = a
        args.append(nc.dram_tensor(f"in_{name}", a.shape, mybir.dt.from_np(a.dtype), kind="ExternalInput").ap())
    out = nc.dram_tensor("out_h", [SEQ, D_MODEL], F32, kind="ExternalOutput").ap()
    hybrid_block(nc, *args, out)
    r = run_bass_kernel_spmd(nc, [arrays], core_ids=[0])
    return r.results[0]["out_h"].reshape(1, SEQ, D_MODEL)
```
